# Optimizing a Trainium2 kernel written in Bass

```python
import math
import jax, jax.numpy as jnp
from jax import lax
import numpy as np

D_MODEL = 1024
BATCH = 1
SEQ = 256
DEPTH = 2
DEC_BATCH = 1
DEC_SEQ = 1024
PAST_LEN = 128

HEAD_DIM = 64
D_MIX = D_MODEL
D_DIL = 3 * D_MIX // 8
D_NA = D_MIX // 4
D_CONV = D_MIX - D_DIL - D_NA
N_DIL_HEADS = D_DIL // HEAD_DIM
N_NA_HEADS = D_NA // HEAD_DIM
D_IN = 3 * D_MIX
CONV_WIDTH = 3
DIL_BRANCHES = ((128, 1), (512, 4), (2048, 16))
DIL_BLOCK = 128
GRID_W = 64
NA_ROWS = 8
NA_COLS = 16
NA_COL_BLOCK = 16
NA_KEY_COLS = 32
ROPE_THETA = 10000.0
D_FF = -(-8 * D_MODEL // (3 * 256)) * 256
RMS_EPS = 1e-6

kernel_name = 'hybrid_bidir_conv_dilated_natten_encoder'

def rmsnorm(x, g):
    xf = x.astype(jnp.float32)
    y = xf * lax.rsqrt(jnp.mean(xf * xf, axis=-1, keepdims=True) + RMS_EPS)
    return (y * g.astype(jnp.float32)).astype(x.dtype)

def rope(x, pos):
    hd = x.shape[-1]
    inv = 1.0 / (ROPE_THETA ** (jnp.arange(0, hd, 2, dtype=jnp.float32) / hd))
    ang = pos[:, None] * inv[None, :]
    cos = jnp.cos(ang)[None, :, None, :]
    sin = jnp.sin(ang)[None, :, None, :]
    x1, x2 = jnp.split(x.astype(jnp.float32), 2, axis=-1)
    out = jnp.concatenate([x1 * cos - x2 * sin, x1 * sin + x2 * cos], axis=-1)
    return out.astype(x.dtype)

def masked_softmax(scores, mask):
    s = jnp.where(mask, scores, -jnp.inf)
    lse = jax.nn.logsumexp(s, axis=-1, keepdims=True)
    return jnp.exp(s - lse), lse[..., 0]

def dilated_branch(q, k, v, window, dilation):
    b, h, s, hd = q.shape
    half = window // (2 * dilation)
    L = s // dilation
    qb = math.gcd(L, DIL_BLOCK)
    nb = L // qb
    klen = qb + 2 * half

    def residues(t):
        return t.reshape(b, h, L, dilation, hd).swapaxes(2, 3)

    qr = residues(q).reshape(b, h, dilation, nb, qb, hd)
    pad = ((0, 0), (0, 0), (0, 0), (half, half), (0, 0))
    kp = jnp.pad(residues(k), pad)
    vp = jnp.pad(residues(v), pad)
    blk = np.arange(nb)
    kk = np.arange(klen)
    qq = np.arange(qb)
    idx = blk[:, None] * qb + kk[None, :]
    kw = kp[:, :, :, idx, :]
    vw = vp[:, :, :, idx, :]
    scores = jnp.einsum('bhrnqe,bhrnke->bhrnqk', qr, kw,
                        preferred_element_type=jnp.float32) * (hd ** -0.5)
    off = kk[None, :] - half - qq[:, None]
    key_pos = idx - half
    mask = (np.abs(off) <= half)[None] & ((key_pos >= 0) & (key_pos < L))[:, None, :]
    p, lse = masked_softmax(scores, mask)
    out = jnp.einsum('bhrnqk,bhrnke->bhrnqe', p.astype(v.dtype), vw,
                     preferred_element_type=jnp.float32)
    out = out.reshape(b, h, dilation, L, hd).swapaxes(2, 3).reshape(b, h, s, hd)
    lse = lse.reshape(b, h, dilation, L).swapaxes(2, 3).reshape(b, h, s)
    return out, lse

def dilated_attention(q, k, v):
    outs, lses = [], []
    for window, dilation in DIL_BRANCHES:
        o, l = dilated_branch(q, k, v, window, dilation)
        outs.append(o)
        lses.append(l)
    w = jax.nn.softmax(jnp.stack(lses, axis=0), axis=0)
    return jnp.einsum('gbhs,gbhse->bhse', w, jnp.stack(outs, axis=0))

def neighbourhood_attention(q, k, v, rpb):
    b, h, s, hd = q.shape
    rows = s // GRID_W
    wr = min(NA_ROWS, rows)
    ncb = GRID_W // NA_COL_BLOCK
    nk = wr * NA_KEY_COLS
    r = np.arange(rows)
    row_start = np.clip(r - wr // 2, 0, rows - wr)
    key_rows = row_start[:, None] + np.arange(wr)
    c0 = np.arange(ncb) * NA_COL_BLOCK
    kc0 = np.clip(c0 - NA_COLS // 2, 0, GRID_W - NA_KEY_COLS)
    key_cols = kc0[:, None] + np.arange(NA_KEY_COLS)
    key_idx = (key_rows[:, None, :, None] * GRID_W
               + key_cols[None, :, None, :]).reshape(rows, ncb, nk)
    kg = k[:, :, key_idx, :]
    vg = v[:, :, key_idx, :]
    qg = q.reshape(b, h, rows, ncb, NA_COL_BLOCK, hd)
    scores = jnp.einsum('bhrcqe,bhrcke->bhrcqk', qg, kg,
                        preferred_element_type=jnp.float32) * (hd ** -0.5)
    qc = c0[:, None] + np.arange(NA_COL_BLOCK)
    col_start = np.clip(qc - NA_COLS // 2, 0, GRID_W - NA_COLS)
    kcol = np.broadcast_to(key_cols[:, None, :], (ncb, wr, NA_KEY_COLS)).reshape(ncb, nk)
    col_ok = (kcol[:, None, :] >= col_start[:, :, None]) & (kcol[:, None, :] < col_start[:, :, None] + NA_COLS)
    drow = np.broadcast_to(key_rows[:, :, None] - r[:, None, None], (rows, wr, NA_KEY_COLS)).reshape(rows, nk)
    dcol = kcol[:, None, :] - qc[:, :, None]
    ri = drow + NA_ROWS - 1
    ci = np.clip(dcol + NA_COLS - 1, 0, 2 * NA_COLS - 2)
    bias = rpb[:, ri[:, None, None, :], ci[None, :, :, :]]
    scores = scores + bias[None].astype(jnp.float32)
    p, _ = masked_softmax(scores, col_ok)
    out = jnp.einsum('bhrcqk,bhrcke->bhrcqe', p.astype(v.dtype), vg,
                     preferred_element_type=jnp.float32)
    return out.reshape(b, h, s, hd)

def short_conv_mixer(gate_b, gate_c, h_in, conv_w):
    u = gate_c * h_in
    conv = lax.conv_general_dilated(
        u, conv_w[:, None, :].astype(u.dtype), window_strides=(1,),
        padding=((CONV_WIDTH // 2, CONV_WIDTH // 2),),
        dimension_numbers=('NWC', 'WIO', 'NWC'), feature_group_count=u.shape[-1])
    return gate_b * conv

def encoder_layer(x, g_pre_mix, w_in, conv_w, rpb, w_out, g_post_mix,
                  g_pre_ffn, w_gate, w_up, w_down, g_post_ffn):
    b, s, _ = x.shape
    hn = rmsnorm(x, g_pre_mix)
    proj = hn @ w_in
    sizes = [D_DIL] * 3 + [D_NA] * 3 + [D_CONV] * 3
    cuts = list(np.cumsum(sizes)[:-1])
    q_d, k_d, v_d, q_n, k_n, v_n, gate_b, gate_c, h_in = jnp.split(proj, cuts, axis=-1)

    pos = jnp.arange(s, dtype=jnp.float32)
    heads = lambda t, n: t.reshape(b, s, n, HEAD_DIM)
    to_bhsd = lambda t: t.transpose(0, 2, 1, 3)
    qd = to_bhsd(rope(heads(q_d, N_DIL_HEADS), pos))
    kd = to_bhsd(rope(heads(k_d, N_DIL_HEADS), pos))
    vd = to_bhsd(heads(v_d, N_DIL_HEADS))
    y_dil = dilated_attention(qd, kd, vd).astype(x.dtype)
    y_dil = y_dil.transpose(0, 2, 1, 3).reshape(b, s, D_DIL)

    qn = to_bhsd(heads(q_n, N_NA_HEADS))
    kn = to_bhsd(heads(k_n, N_NA_HEADS))
    vn = to_bhsd(heads(v_n, N_NA_HEADS))
    y_na = neighbourhood_attention(qn, kn, vn, rpb).astype(x.dtype)
    y_na = y_na.transpose(0, 2, 1, 3).reshape(b, s, D_NA)

    y_conv = short_conv_mixer(gate_b, gate_c, h_in, conv_w)

    mixed = jnp.concatenate([y_dil, y_na, y_conv], axis=-1) @ w_out
    x = x + rmsnorm(mixed, g_post_mix)

    hf = rmsnorm(x, g_pre_ffn)
    f = (jax.nn.silu(hf @ w_gate) * (hf @ w_up)) @ w_down
    return x + rmsnorm(f, g_post_ffn)

def setup_inputs(seed: int = 0) -> dict:
    key = jax.random.key(seed)
    ks = jax.random.split(key, 14)
    nrm = lambda k, shape, scale: jax.random.normal(k, shape, jnp.float32) * scale
    gain = lambda k: 1.0 + 0.05 * jax.random.normal(k, (DEPTH, D_MODEL), jnp.float32)
    return {
        'x_prompt': nrm(ks[0], (BATCH, SEQ, D_MODEL), 1.0),
        'x_sample': nrm(ks[1], (DEC_BATCH, DEC_SEQ, D_MODEL), 1.0),
        'g_pre_mix': gain(ks[2]),
        'w_in': nrm(ks[3], (DEPTH, D_MODEL, D_IN), D_MODEL ** -0.5),
        'conv_w': nrm(ks[4], (DEPTH, CONV_WIDTH, D_CONV), CONV_WIDTH ** -0.5),
        'rpb': nrm(ks[5], (DEPTH, N_NA_HEADS, 2 * NA_ROWS - 1, 2 * NA_COLS - 1), 0.2),
        'w_out': nrm(ks[6], (DEPTH, D_MIX, D_MODEL), D_MIX ** -0.5),
        'g_post_mix': gain(ks[7]),
        'g_pre_ffn': gain(ks[8]),
        'w_gate': nrm(ks[9], (DEPTH, D_MODEL, D_FF), D_MODEL ** -0.5),
        'w_up': nrm(ks[10], (DEPTH, D_MODEL, D_FF), D_MODEL ** -0.5),
        'w_down': nrm(ks[11], (DEPTH, D_FF, D_MODEL), D_FF ** -0.5),
        'g_post_ffn': gain(ks[12]),
    }

def reference(x_prompt, x_sample, g_pre_mix, w_in, conv_w, rpb, w_out, g_post_mix,
              g_pre_ffn, w_gate, w_up, w_down, g_post_ffn):
    y_prompt = x_prompt
    y_sample = x_sample
    for l in range(DEPTH):
        y_prompt = encoder_layer(y_prompt, g_pre_mix[l], w_in[l], conv_w[l], rpb[l], w_out[l],
                                 g_post_mix[l], g_pre_ffn[l], w_gate[l], w_up[l], w_down[l],
                                 g_post_ffn[l])
        y_sample = encoder_layer(y_sample, g_pre_mix[l], w_in[l], conv_w[l], rpb[l], w_out[l],
                                 g_post_mix[l], g_pre_ffn[l], w_gate[l], w_up[l], w_down[l],
                                 g_post_ffn[l])
    return (y_prompt, y_sample)


_drawn_inputs = setup_inputs


def setup_inputs(seed=0):
    import zlib

    import numpy as np

    out = dict(_drawn_inputs(seed))
    spreads = {}
    factors = {}
    for name, (base, spread) in spreads.items():
        noise = np.random.default_rng([zlib.crc32(name.encode()), seed]).standard_normal(out[name].shape)
        drawn = base * np.exp(spread * noise) if base else spread * noise
        out[name] = __import__('jax').numpy.asarray(drawn.astype(out[name].dtype))
    for name, factor in factors.items():
        out[name] = (out[name] * factor).astype(out[name].dtype)
    return out
```

```python
from contextlib import ExitStack

import numpy as np

import concourse.bass as bass
from concourse import mybir

F32 = mybir.dt.float32
F32R = mybir.dt.float32r
ALU = mybir.AluOpType
ACT = mybir.ActivationFunctionType

P = 128
DEPTH = 2
D = 1024
KT = D // P
S_SAMPLE, S_PROMPT = 1024, 256
T = S_SAMPLE + S_PROMPT
CHUNKS = ((0, 512), (512, 512), (1024, 256))
NCH = len(CHUNKS)
TILES = T // P
HD = 64
D_DIL, D_NA, D_CONV = 384, 256, 384
D_IN = 3 * D
D_FF = 2816
FT = D_FF // P
GRID_W, NA_ROWS, NA_COLS = 64, 8, 16
EPS = 1e-6
MASKED = -1e30
SCALE = HD ** -0.5

DIL_UNITS = [(i, h, 0, 8) for i in range(8) for h in range(2)] + \
            [(i, h, 8, 2) for i in (8, 9) for h in range(2)]


def na_keys(i):
    if i >= 8:
        return 8, 2
    if i < 2:
        return 0, 4
    if i >= 6:
        return 4, 4
    return i - 2, 5


NA_UNITS = [(i, h) + na_keys(i) for i in range(TILES) for h in range(2)]


def quads(nkt):
    return [(a, min(4, nkt - a)) for a in range(0, nkt, 4)]


N_DQ = sum(len(quads(u[3])) for u in DIL_UNITS)
N_NQ = sum(len(quads(u[3])) for u in NA_UNITS)
NU = len(DIL_UNITS)

ATT = dict(scored=NU, masked=NU, exped=NU, pv=NU, o_tmp=NU, recip=NU, y=NU, yt=TILES, yb=TILES,
           yout=1, vt=3, vh=3, vl=3, stack_hi=6, stack_lo=6)
UPDATE = dict(sq=48, part=48, sumd=6, rooted=6, rstd=6, z=72, xh=24, xl=24)
PER = {
    "layer0": dict(gains=1, tab=1),
    "dil": dict(trip=1, unit=3, gained=3, group=9, tp=N_DQ, pth=N_DQ, ptl=N_DQ, swap=8, cell=10,
                **ATT),
    "na": dict(trip=1, unit=3, gained=3, group=9, tp=N_NQ, pth=N_NQ, ptl=N_NQ, cell=5, bias_in=4,
               **ATT),
    "conv": dict(trip=1, unit=3, gained=3, group=9, cell=8, yout=1, cw=1, yb=2),
    "out": dict(trip=8, unit=24, group=24, mload=3, mhi=24, mlo=24, **UPDATE),
    "ffn0": dict(unit=1, gained=1, group=3, gate=3, sig=3, sgr=3),
    "ffn": dict(trip=2, unit=6, gained=4, group=36, gate=6, sig=6, sgr=6, h=6, hh=6, hl=6),
    "ffn1": dict(unit=5, gained=3, group=33, gate=3, sig=3, sgr=3, h=6, hh=6, hl=6),
    "upd": dict(trip=2, cleared=1, **UPDATE),
}
COUNT = {"layer0": 1, "dil": 3, "na": 2, "conv": 3, "out": 1, "ffn0": 1, "ffn": 10, "ffn1": 1,
         "upd": 1}
FIRST = dict(used=3, drained=3, lo=3, cell=1, yout=1, sq=24, part=24, sumd=3, rooted=3, rstd=3, xh=24, xl=24)
SAME = {"hi": "unit", "lo": "unit", "used": "unit", "drained": "group"}
ORDER = list(PER)


class At:

    def __init__(self, layer):
        self.base = {}
        self.names = {k for p in PER.values() for k in p} | set(SAME)
        for k in self.names:
            per = sum(PER[s].get(SAME.get(k, k), 0) * COUNT[s] for s in ORDER)
            self.base[k] = layer * per + FIRST.get(k, 0)

    def __getitem__(self, k):
        return self.base[k]

    def step(self, section, times=1):
        for k in self.names:
            self.base[k] = self.base[k] + times * PER[section].get(SAME.get(k, k), 0)

    def body(self, section, it):
        new = At.__new__(At)
        new.names = self.names
        new.base = {k: self.base[k] + it * PER[section].get(SAME.get(k, k), 0)
                    if PER[section].get(SAME.get(k, k), 0) else self.base[k] for k in self.names}
        return new


def constants():
    f = np.float32
    inv = (f(1.0) / (f(10000.0) ** (np.arange(0, HD, 2, dtype=f) / f(HD)))).astype(f)
    ang = (np.arange(S_SAMPLE, dtype=f)[None, :] * inv[:, None]).astype(f)
    cos, sin = np.cos(ang).astype(f), np.sin(ang).astype(f)
    cos128 = np.concatenate([cos] * 4, 0)
    sin128 = np.concatenate([-sin, sin, -sin, sin], 0)
    d = np.abs(np.arange(1920)[None, :] - 896 - np.arange(P)[:, None])
    count = (d <= 64).astype(int) + ((d % 4 == 0) & (d <= 256)) + (d % 16 == 0)
    log = np.where(count > 0, np.log(np.maximum(count, 1)), MASKED).astype(f)
    qc = np.arange(GRID_W)
    start = np.clip(qc - NA_COLS // 2, 0, GRID_W - NA_COLS)
    ok = (qc[None, :] >= start[:, None]) & (qc[None, :] < start[:, None] + NA_COLS)
    cmask = np.tile(np.where(ok, 0.0, MASKED).astype(f), (2, 1))
    eye_ones = np.concatenate([np.eye(P, dtype=f), np.ones((P, P), f), cmask], 1)
    return np.ascontiguousarray(np.concatenate([log, cos128, sin128], 1)), eye_ones


def build(nc, x, w_in, w_out, w_gate, w_up, w_down, gains, conv_w, rpb, tables, small, mixed, out):
    with ExitStack() as ctx:
        at = [4096]

        def place(name, shape, dt=F32, offset=None):
            size = int(np.prod(shape[1:])) * 4
            if offset is None:
                offset, at[0] = at[0], at[0] + (size + 31) // 32 * 32
            return nc.alloc_sbuf_tensor_at(name, shape, dt, offset=offset)

        XH = place("XH", [P, KT, T], F32R)
        XL = place("XL", [P, KT, T], F32R)
        RS = place("RS", [P, T])
        RAW = [place(f"RAW{s}", [P, KT, P]) for s in range(3)]
        WH, WL = [], []
        for s in range(4):
            WH.append(place(f"WH{s}", [P, KT, P], F32R))
            WL.append(place(f"WL{s}", [P, KT, P], F32R))
        w3 = at[0] - 8192
        EYE = place("EYE", [P, 2 * P + GRID_W])
        ident, ones, cmask = EYE[:, 0:P], EYE[:, P:2 * P], EYE[:, 2 * P:]
        GL = place("GL", [P, 4 * KT])
        CW = place("CW", [P, 3])
        EPSC = place("EPSC", [P, 1])
        base = at[0]
        NM = place("NM", [P, 4])
        SM = place("SM", [P, 4])
        RC = place("RC", [P, 4])
        OT = place("OT", [P, 2, HD])
        YN = place("YN", [P, 2, P])
        QS = [place(f"QS{h}", [P, T], F32R) for h in range(2)]
        KH = [place(f"KH{h}", [P, T], F32R) for h in range(2)]
        KL = [place(f"KL{h}", [P, T], F32R) for h in range(2)]
        TA = place("TA", [P, T])
        TB = place("TB", [P, T])
        TC = place("TC", [P, T])
        V = place("V", [P, TILES, 2, P], F32R)
        PR = place("PR", [P, 2, 1024])
        YB = place("YB", [P, T])
        tab = at[0]
        TAB = place("TAB", [P, 1920 + 2 * 1024])
        assert at[0] <= 229247, at[0]
        EB = place("EB", [P, 2, 14, GRID_W], offset=tab)
        IB = place("IB", [P, 2, 10, GRID_W], offset=tab + 7168)
        U = place("U", [P, T + 4], offset=tab)
        CV = place("CV", [P, T + 4], offset=tab + 5184)
        PTH = place("PTH", [P, 2, 4, P], F32R, offset=w3)
        PTL = place("PTL", [P, 2, 4, P], F32R, offset=w3 + 4096)
        at[0] = base
        SQ = place("SQ", [P, 2, 512])
        SSA = place("SSA", [P, 512])
        RT = place("RT", [P, 512])
        R2 = place("R2", [P, 512])
        past_norms = at[0]
        MS = place("MS", [P, KT, 512])
        MH = place("MH", [P, KT, 512], F32R)
        ML = place("ML", [P, KT, 512], F32R)
        Y2 = place("Y2", [P, KT, 512])
        assert at[0] <= 229247, at[0]
        at[0] = past_norms
        ACC = place("ACC", [P, KT, T])
        past_acc = at[0]
        HH = [place(f"HH{j}", [P, T], F32R) for j in range(2)]
        HL = [place(f"HL{j}", [P, T], F32R) for j in range(2)]
        SG = place("SG", [P, T])
        HT = place("HT", [P, 2, 512])
        assert at[0] <= 229247, at[0]
        ZO = place("ZO", [P, 2, D], offset=past_acc)
        XIN = place("XIN", [P, TILES, D], offset=past_norms)

        PS = ctx.enter_context(nc.psum_tensor("PS", [P, 8, 512], F32))

        def sem(name):
            return ctx.enter_context(nc.semaphore(name))

        s_consts = sem("consts")
        s_xin = sem("xin")
        s_turned = sem("turned")
        s_started = sem("started")
        s_gains = sem("gains")
        s_tab = sem("tab")
        s_bias_in = sem("bias_in")
        s_cw = sem("cw")
        s_load0 = sem("load0")
        s_load1 = sem("load1")
        s_load2 = sem("load2")
        s_gained = sem("gained")
        s_hi = sem("hi")
        s_lo = sem("lo")
        s_used = sem("used")
        s_group = sem("group")
        s_drained = sem("drained")
        s_xh = sem("xh")
        s_xl = sem("xl")
        s_sq = sem("sq")
        s_part = sem("part")
        s_sumd = sem("sumd")
        s_rooted = sem("rooted")
        s_rstd = sem("rstd")
        s_z = sem("z")
        s_cell = sem("cell")
        s_swap = sem("swap")
        s_stack_hi = sem("stack_hi")
        s_stack_lo = sem("stack_lo")
        s_mask_may = sem("mask_may")
        s_clear_may = sem("clear_may")
        s_vt = sem("vt")
        s_vh = sem("vh")
        s_vl = sem("vl")
        s_scored = sem("scored")
        s_masked = sem("masked")
        s_exped = sem("exped")
        s_tp = sem("tp")
        s_pth = sem("pth")
        s_ptl = sem("ptl")
        s_pv = sem("pv")
        s_o_tmp = sem("o_tmp")
        s_recip = sem("recip")
        s_y = sem("y")
        s_yt = sem("yt")
        s_yb = sem("yb")
        s_yout = sem("yout")
        s_mload = sem("mload")
        s_mhi = sem("mhi")
        s_mlo = sem("mlo")
        s_gate = sem("gate")
        s_sig = sem("sig")
        s_sgr = sem("sgr")
        s_h = sem("h")
        s_hh = sem("hh")
        s_hl = sem("hl")
        s_cleared = sem("cleared")
        s_zt = sem("zt")
        s_zo = sem("zo")
        s_zout0 = sem("zout0")
        s_zout1 = sem("zout1")
        loads = (s_load0, s_load1, s_load2)
        zouts = (s_zout0, s_zout1)

        wv = {k: w.rearrange("l (t p) n -> l p t n", p=P)
              for k, w in (("in", w_in), ("out", w_out), ("gate", w_gate), ("up", w_up))}

        block = ctx.enter_context(nc.Block())

        @block.sync
        def _(sp):
            sp.dma_start(EYE[:, :], small).then_inc(s_consts, 16)
            for i in range(TILES):
                sp.dma_start(XIN[:, i, :], x[i * P:(i + 1) * P, :]).then_inc(s_xin, 16)

            def load(at, k, matrix, L, col, ring=0):
                slot = (ring + k) % 3
                sp.wait_ge(s_lo, at["lo"] + (k - 2))
                src = wv[matrix][bass.ds(L, 1), :, :, bass.ds(col, P)]
                sp.dma_start(RAW[slot][:, :, :], src.rearrange("l p t n -> (l p) t n")) \
                    .then_inc(loads[slot], 16)

            def load_down(at, k, L, row):
                slot = (1 + k) % 3
                sp.wait_ge(s_lo, at["lo"] + (k - 2))
                sp.dma_start(RAW[slot][:, :, :].rearrange("p t n -> p (t n)"),
                             w_down[bass.ds(L, 1), bass.ds(row, P), :]
                             .rearrange("l p n -> (l p) n")).then_inc(loads[slot], 16)

            with sp.Fori(0, DEPTH) as L:
                at = At(L)
                sp.wait_ge(s_xl, at["xl"])
                sp.dma_start(GL[:, :], gains[bass.ds(L, 1), :, :].rearrange("l p n -> (l p) n")) \
                    .then_inc(s_gains, 16)
                sp.dma_start(TAB[:, :], tables).then_inc(s_tab, 16)
                at.step("layer0")
                with sp.Fori(0, 3) as j:
                    b = at.body("dil", j)
                    for k in range(3):
                        load(b, k, "in", L, j * P + k * D_DIL)
                at.step("dil", 3)
                with sp.Fori(0, 2) as j:
                    b = at.body("na", j)
                    load(b, 0, "in", L, j * P + 3 * D_DIL)
                    sp.wait_ge(s_masked, b["masked"])
                    for half in range(2):
                        rows = slice(1, 15) if half == 0 else slice(0, 14)
                        for h in range(2):
                            sp.dma_start(
                                EB[64 * half:64 * half + 64, h, :, :],
                                rpb[bass.ds(L, 1), bass.ds(j * 2 + h, 1), :, rows, :]
                                .rearrange("l h q r k -> (l h q) r k")).then_inc(s_bias_in, 16)
                    load(b, 1, "in", L, j * P + 3 * D_DIL + D_NA)
                    load(b, 2, "in", L, j * P + 3 * D_DIL + 2 * D_NA)
                at.step("na", 2)
                with sp.Fori(0, 3) as j:
                    b = at.body("conv", j)
                    sp.wait_ge(s_cell, b["cell"])
                    sp.dma_start(CW[:, :], conv_w[bass.ds(L, 1), bass.ds(j, 1), :, :]
                                 .rearrange("l c p w -> (l c p) w")).then_inc(s_cw, 16)
                    for k, part in enumerate((1, 2, 0)):
                        load(b, k, "in", L, j * P + (3 * D_DIL + 3 * D_NA + part * D_CONV))
                at.step("conv", 3)
                for c, (t0, n) in enumerate(CHUNKS):
                    if c == 0:
                        sp.wait_ge(s_yout, 16 * at["yout"])
                    else:
                        sp.wait_ge(s_mlo, at["mlo"] + 8 * c)
                    sp.dma_start(MS[:, :, 0:n], mixed[:, :, t0:t0 + n].rearrange("b p n -> p b n")) \
                        .then_inc(s_mload, 16)
                    for nb in range(KT):
                        load(at, 8 * c + nb, "out", L, nb * P)
                at.step("out")
                load(at, 0, "gate", L, 0)
                at.step("ffn0")
                with sp.Fori(0, 10) as j:
                    b = at.body("ffn", j)
                    for k, (m, f) in enumerate((("up", 0), ("gate", 1), ("up", 1), ("gate", 2))):
                        load(b, k, m, L, j * (2 * P) + f * P, ring=1)
                    for k in range(2):
                        load_down(b, 4 + k, L, j * (2 * P) + k * P)
                at.step("ffn", 10)
                for k, (m, f) in enumerate((("up", 20), ("gate", 21), ("up", 21))):
                    load(at, k, m, L, f * P, ring=1)
                for k in range(2):
                    load_down(at, 3 + k, L, (20 + k) * P)
                at.step("ffn1")
                at.step("upd")
            for i in range(TILES):
                sp.wait_ge(s_zo, 2 * i + 2)
                sp.dma_start(out[i * P:(i + 1) * P, :], ZO[:, i % 2, :]).then_inc(zouts[i % 2], 16)
            for half in range(2):
                sp.wait_ge(zouts[half], 16 * (TILES // 2))

        @block.gpsimd
        def _(pool):
            def gain(at, k, g, which, ring=0):
                slot = (ring + k) % 3
                pool.wait_ge(loads[slot], 16 * (at["trip"] + ((ring + k) // 3 + 1)))
                gcol = GL[:, which * KT:which * KT + KT].unsqueeze(2).to_broadcast([P, KT, P])
                nc.gpsimd.tensor_tensor(RAW[slot][:, :, :], RAW[slot][:, :, :], gcol, ALU.mult) \
                    .then_inc(s_gained, 1)

            def low(at, k, slot_w, ring=0):
                slot = (ring + k) % 3
                pool.wait_ge(s_hi, at["hi"] + (k + 1))
                nc.gpsimd.tensor_tensor(WL[slot_w][:, :, :], RAW[slot][:, :, :],
                                        WH[slot_w][:, :, :].bitcast(F32), ALU.subtract) \
                    .then_inc(s_lo, 1)

            def add_squares(sq0, part0, event, n):
                for i in range(1, KT):
                    pool.wait_ge(s_sq, sq0 + (i + 1))
                    if i == 1:
                        pool.wait_ge(s_sumd, event)
                        nc.gpsimd.tensor_tensor(SSA[:, 0:n], SQ[:, 0, 0:n], SQ[:, 1, 0:n],
                                                ALU.add).then_inc(s_part, 2)
                    else:
                        pool.wait_ge(s_part, part0 + i)
                        nc.gpsimd.tensor_tensor(SSA[:, 0:n], SSA[:, 0:n], SQ[:, i % 2, 0:n],
                                                ALU.add).then_inc(s_part, 1)

            def update(at):
                for c, (t0, n) in enumerate(CHUNKS):
                    update_chunk(at, c)

            def update_chunk(at, c):
                n = CHUNKS[c][1]
                for e in (2 * c, 2 * c + 1):
                    add_squares(at["sq"] + 8 * e, at["part"] + 8 * e, at["sumd"] + e, n)

            pool.sem_inc(s_lo, 3)
            for c, (t0, n) in enumerate(CHUNKS):
                add_squares(8 * c, 8 * c, c, n)
            with pool.Fori(0, DEPTH) as L:
                at = At(L)
                at.step("layer0")
                for section, times in (("dil", 3), ("na", 2), ("conv", 3)):
                    with pool.Fori(0, times) as j:
                        b = at.body(section, j)
                        pool.wait_ge(s_gains, 16 * b["gains"])
                        for k in range(3):
                            gain(b, k, k, 0)
                            low(b, k, k)
                    at.step(section, times)
                for c in range(NCH):
                    for nb in range(KT):
                        low(at, 8 * c + nb, (8 * c + nb) % 3)
                    update_chunk(at, c)
                at.step("out")

                def scaled_gate(at, i, c):
                    t0, n = CHUNKS[c]
                    pool.wait_ge(s_sig, at["sig"] + (i + 1))
                    nc.gpsimd.tensor_tensor(SG[:, t0:t0 + n], SG[:, t0:t0 + n], RS[:, t0:t0 + n],
                                            ALU.mult).then_inc(s_sgr, 1)

                gain(at, 0, 0, 2)
                low(at, 0, 0)
                pool.wait_ge(s_xl, at["xl"])
                pool.sem_inc(s_clear_may, 1)
                nc.gpsimd.memset(ACC[:, :, :], 0.0).then_inc(s_cleared, 1)
                for c in range(NCH):
                    scaled_gate(at, c, c)
                at.step("ffn0")
                with pool.Fori(0, 10) as j:
                    b = at.body("ffn", j)
                    for k, w in ((0, 1), (1, 0), (2, 1)):
                        gain(b, k, k, 2, ring=1)
                        low(b, k, w, ring=1)
                    for c in range(NCH):
                        scaled_gate(b, c, c)
                    gain(b, 3, 3, 2, ring=1)
                    low(b, 3, 0, ring=1)
                    low(b, 4, 2, ring=1)
                    low(b, 5, 3, ring=1)
                    for c in range(NCH):
                        scaled_gate(b, 3 + c, c)
                at.step("ffn", 10)
                for k, w in ((0, 1), (1, 0), (2, 1)):
                    gain(at, k, k, 2, ring=1)
                    low(at, k, w, ring=1)
                for c in range(NCH):
                    scaled_gate(at, c, c)
                low(at, 3, 2, ring=1)
                low(at, 4, 3, ring=1)
                at.step("ffn1")
                update(at)
                at.step("upd")

        @block.scalar
        def _(act):
            def high(at, k, slot_w, gained=None, ring=0, back=3):
                slot = (ring + k) % 3
                if gained is None:
                    act.wait_ge(loads[slot], 16 * (at["trip"] + ((ring + k) // 3 + 1)))
                else:
                    act.wait_ge(s_gained, at["gained"] + (gained + 1))
                act.wait_ge(s_used, at["used"] + (k - back + 1))
                nc.scalar.activation(WH[slot_w][:, :, :], RAW[slot][:, :, :], ACT.Copy) \
                    .then_inc(s_hi, 1)

            def square(src, i, n, part):
                if i >= 2:
                    act.wait_ge(s_part, part + (i - 1))
                nc.scalar.activation(SQ[:, i % 2, 0:n], src, ACT.Square).then_inc(s_sq, 1)

            def root(event, n):
                act.wait_ge(s_sumd, event + 1)
                act.wait_ge(s_rstd, event)
                nc.scalar.activation(RT[:, 0:n], PS[:, 7, 0:n], ACT.Sqrt, scale=1.0 / D, bias=EPSC[:, 0:1]) \
                    .then_inc(s_rooted, 1)

            def update_chunk(at, c, Y, t_y, ready, ready_at):
                t0, n = CHUNKS[c]
                e = 2 * c
                act.wait_ge(ready, ready_at)
                act.wait_ge(s_part, at["part"] + 8 * e)
                for i in range(KT):
                    square(Y[:, i, t_y:t_y + n], i, n, at["part"] + 8 * e)
                root(at["rooted"] + e, n)
                e += 1
                act.wait_ge(s_part, at["part"] + 8 * e)
                for i in range(KT):
                    act.wait_ge(s_z, at["z"] + 24 * c + 3 * (i + 1))
                    nc.scalar.activation(XH[:, i, t0:t0 + n], Y[:, i, t_y:t_y + n], ACT.Copy) \
                        .then_inc(s_xh, 1)
                    square(Y[:, i, t_y:t_y + n], i, n, at["part"] + 8 * e)
                root(at["rooted"] + e, n)

            act.wait_ge(s_started, 1)
            for c, (t0, n) in enumerate(CHUNKS):
                act.wait_ge(s_part, 8 * c)
                for i in range(KT):
                    act.wait_ge(s_turned, 8 * c + i + 1)
                    nc.scalar.activation(XH[:, i, t0:t0 + n], PS[:, i % 6, 0:n], ACT.Copy) \
                        .then_inc(s_xh, 1)
                    square(PS[:, i % 6, 0:n], i, n, 8 * c)
                root(c, n)

            def split_q(b, src_ready):
                src_ready()
                nc.scalar.activation(QS[0][0:64, :], TA[0:64, :], ACT.Copy).then_inc(s_stack_hi, 1)
                nc.scalar.activation(QS[1][64:128, :], TA[64:128, :], ACT.Copy) \
                    .then_inc(s_stack_hi, 1)

            def split_k(b, src_ready):
                src_ready()
                for h in range(2):
                    own = TB[64 * h:64 * h + 64, :]
                    for half in (h, 1 - h):
                        nc.scalar.activation(KH[h][64 * half:64 * half + 64, :], own, ACT.Copy) \
                            .then_inc(s_stack_hi, 1)

            def swap_halves(b, src, group, cell):
                act.wait_ge(s_drained, b["drained"] + group)
                act.wait_ge(s_cell, b["cell"] + cell)
                for q in range(4):
                    o = q ^ 1
                    nc.scalar.activation(TC[32 * o:32 * o + 32, :], src[32 * q:32 * q + 32, :],
                                         ACT.Copy).then_inc(s_swap, 1)

            def split_v(b):
                for g, (bank, a, n) in enumerate(VBANKS):
                    act.wait_ge(s_vt, b["vt"] + (g + 1))
                    ps = PS[:, bank, 0:n * P].rearrange("p (t h d) -> p t h d", h=2, d=HD)
                    nc.scalar.activation(V[:, a:a + n, :, 0:HD], ps, ACT.Copy).then_inc(s_vh, 1)

            def attention(b, units):
                starts = quad_starts(units)

                def exp(u):
                    i, h, k0, nkt = units[u]
                    act.wait_ge(s_masked, b["masked"] + (u + 1))
                    nc.scalar.activation(PR[:, u % 2, 0:nkt * P], PR[:, u % 2, 0:nkt * P], ACT.Exp,
                                         scale=-1.0, bias=NM[:, u % 4:u % 4 + 1],
                                         accum_out=SM[:, u % 4:u % 4 + 1]).then_inc(s_exped, 1)

                def o_low(u):
                    act.wait_ge(s_pv, b["pv"] + (u + 1))
                    act.wait_ge(s_recip, b["recip"] + (u + 1))
                    if u >= 2:
                        act.wait_ge(s_y, b["y"] + (u - 1))
                    nc.scalar.activation(OT[:, u % 2, :], PS[:, 6 + u % 2, HD:P],
                                         ACT.Copy, scale=RC[:, u % 4:u % 4 + 1]) \
                        .then_inc(s_o_tmp, 1)

                def y_block(i):
                    act.wait_ge(s_yt, b["yt"] + (i + 1))
                    if i == 0:
                        act.wait_ge(s_yout, 16 * b["yout"])
                    nc.scalar.activation(YB[:, i * P:(i + 1) * P],
                                         PS[:, 7, 0:P], ACT.Copy) \
                        .then_inc(s_yb, 1)

                exp(0)
                for u in range(NU + 1):
                    if u + 1 < NU:
                        exp(u + 1)
                    if 1 <= u <= NU:
                        o_low(u - 1)
                    if u < NU:
                        for g, (a, n) in enumerate(quads(units[u][3])):
                            act.wait_ge(s_tp, b["tp"] + (starts[u] + g + 1))
                            if u:
                                act.wait_ge(s_pv, b["pv"] + u)
                            nc.scalar.activation(PTH[:, g, 0:n, :].rearrange("p t q -> p (t q)"),
                                                 PS[:, 4 + g, 0:n * P], ACT.Copy) \
                                .then_inc(s_pth, 1)
                    if u >= 2 and u % 2 == 0:
                        y_block(u // 2 - 1)

            def store_block(b, L, block, n_yb):
                act.wait_ge(s_yb, b["yb"] + n_yb)
                act.dma_start(mixed[bass.ds(block, 1), :, :].rearrange("b p n -> (b p) n"),
                              YB[:, :]).then_inc(s_yout, 16)

            with act.Fori(0, DEPTH) as L:
                at = At(L)
                at.step("layer0")
                with act.Fori(0, 3) as j:
                    b = at.body("dil", j)
                    for k in range(3):
                        high(b, k, k, gained=k)
                    swap_halves(b, TA, 3, 0)
                    split_q(b, lambda: act.wait_ge(s_cell, b["cell"] + 5))
                    swap_halves(b, TB, 6, 5)
                    split_k(b, lambda: act.wait_ge(s_cell, b["cell"] + 10))
                    split_v(b)
                    attention(b, DIL_UNITS)
                    store_block(b, L, j, TILES)
                at.step("dil", 3)
                with act.Fori(0, 2) as j:
                    b = at.body("na", j)
                    for k in range(3):
                        high(b, k, k, gained=k)
                    split_q(b, lambda: act.wait_ge(s_drained, b["drained"] + 3))
                    split_k(b, lambda: act.wait_ge(s_drained, b["drained"] + 6))
                    split_v(b)
                    attention(b, NA_UNITS)
                    store_block(b, L, j + 3, TILES)
                at.step("na", 2)
                with act.Fori(0, 3) as j:
                    b = at.body("conv", j)
                    for k in range(3):
                        high(b, k, k, gained=k)
                    store_block(b, L, j + 5, 2)
                at.step("conv", 3)
                for c, (t0, n) in enumerate(CHUNKS):
                    act.wait_ge(s_mload, 16 * (at["mload"] + (c + 1)))
                    act.wait_ge(s_used, at["used"] + 8 * c)
                    for i in range(KT):
                        nc.scalar.activation(MH[:, i, 0:n], MS[:, i, 0:n], ACT.Copy) \
                            .then_inc(s_mhi, 1)
                    for nb in range(KT):
                        high(at, 8 * c + nb, (8 * c + nb) % 3)
                    update_chunk(at, c, Y2, 0, s_drained, at["drained"] + 8 * (c + 1))
                at.step("out")

                def silu(at, i, c):
                    t0, n = CHUNKS[c]
                    act.wait_ge(s_gate, at["gate"] + (i + 1))
                    nc.scalar.activation(SG[:, t0:t0 + n], SG[:, t0:t0 + n], ACT.Silu) \
                        .then_inc(s_sig, 1)

                def hidden_high(at, i, t, c):
                    t0, n = CHUNKS[c]
                    act.wait_ge(s_h, at["h"] + (i + 1))
                    nc.scalar.activation(HH[t][:, t0:t0 + n], HT[:, i % 2, 0:n], ACT.Copy) \
                        .then_inc(s_hh, 1)

                high(at, 0, 0, gained=0)
                for c in range(NCH):
                    silu(at, c, c)
                at.step("ffn0")
                with act.Fori(0, 10) as j:
                    b = at.body("ffn", j)
                    high(b, 0, 1, gained=0, ring=1)
                    high(b, 1, 0, gained=1, ring=1, back=2)
                    for c in range(NCH):
                        hidden_high(b, c, 0, c)
                    high(b, 2, 1, gained=2, ring=1, back=2)
                    for c in range(NCH):
                        silu(b, c, c)
                    high(b, 3, 0, gained=3, ring=1, back=2)
                    high(b, 4, 2, ring=1, back=4)
                    high(b, 5, 3, ring=1, back=5)
                    for c in range(NCH):
                        hidden_high(b, 3 + c, 1, c)
                    for c in range(NCH):
                        silu(b, 3 + c, c)
                at.step("ffn", 10)
                high(at, 0, 1, gained=0, ring=1)
                high(at, 1, 0, gained=1, ring=1, back=2)
                for c in range(NCH):
                    hidden_high(at, c, 0, c)
                high(at, 2, 1, gained=2, ring=1, back=2)
                for c in range(NCH):
                    silu(at, c, c)
                high(at, 3, 2, ring=1)
                high(at, 4, 3, ring=1)
                for c in range(NCH):
                    hidden_high(at, 3 + c, 1, c)
                at.step("ffn1")
                for c, (t0, n) in enumerate(CHUNKS):
                    update_chunk(at, c, ACC, t0, s_drained, at["drained"] - 24 + 8 * (c + 1))
                at.step("upd")
            for i in range(TILES):
                act.wait_ge(s_zt, 2 * i + 2)
                if i >= 2:
                    act.wait_ge(zouts[i % 2], 16 * (i // 2))
                nc.scalar.activation(ZO[:, i % 2, 0:512], PS[:, (2 * i) % 4, :], ACT.Copy) \
                    .then_inc(s_zo, 1)
                nc.scalar.activation(ZO[:, i % 2, 512:1024], PS[:, (2 * i + 1) % 4, :], ACT.Copy) \
                    .then_inc(s_zo, 1)

        @block.vector
        def _(dve):
            def scale_out(b, g, dst, t0, n, bank, factor=None):
                dve.wait_ge(s_group, b["group"] + (g + 1))
                if factor is None:
                    ins = nc.vector.tensor_tensor(dst, PS[:, bank, 0:n], RS[:, t0:t0 + n], ALU.mult)
                else:
                    ins = nc.vector.scalar_tensor_tensor(dst, PS[:, bank, 0:n], factor,
                                                         RS[:, t0:t0 + n], ALU.mult, ALU.mult)
                return ins

            def rope(b, X, block, factor):
                dve.wait_ge(s_tab, 16 * (b["tab"]))
                dve.wait_ge(s_swap, b["swap"] + 4 * (block + 1))
                dve.wait_ge(s_drained, b["drained"] + 3 * (block + 1))
                for Z, col in ((X, 1920), (TC, 1920 + 1024)):
                    for t0, n in ((0, S_SAMPLE), (S_SAMPLE, S_PROMPT)):
                        nc.vector.scalar_tensor_tensor(Z[:, t0:t0 + n], Z[:, t0:t0 + n], factor,
                                                       TAB[:, col:col + n], ALU.mult, ALU.mult) \
                            .then_inc(s_cell, 1)
                dve.wait_ge(s_cell, b["cell"] + (5 * block + 4))
                nc.vector.tensor_tensor(X[:, :], X[:, :], TC[:, :], ALU.add).then_inc(s_cell, 1)

            def split_q(b):
                dve.wait_ge(s_stack_hi, b["stack_hi"] + 2)
                nc.vector.tensor_tensor(QS[0][64:128, :], TA[0:64, :], QS[0][0:64, :].bitcast(F32),
                                        ALU.subtract).then_inc(s_stack_lo, 1)
                nc.vector.tensor_tensor(QS[1][0:64, :], TA[64:128, :],
                                        QS[1][64:128, :].bitcast(F32), ALU.subtract) \
                    .then_inc(s_stack_lo, 1)

            def split_k(b):
                for h in range(2):
                    own = slice(64 * h, 64 * h + 64)
                    dve.wait_ge(s_stack_hi, b["stack_hi"] + 4 + 2 * h)
                    for half in (h, 1 - h):
                        nc.vector.tensor_tensor(KL[h][64 * half:64 * half + 64, :], TB[own, :],
                                                KH[h][own, :].bitcast(F32), ALU.subtract) \
                            .then_inc(s_stack_lo, 1)

            def split_v(b):
                for g, (bank, a, n) in enumerate(VBANKS):
                    dve.wait_ge(s_vh, b["vh"] + (g + 1))
                    ps = PS[:, bank, 0:n * P].rearrange("p (t h d) -> p t h d", h=2, d=HD)
                    nc.vector.tensor_tensor(V[:, a:a + n, :, HD:P], ps,
                                            V[:, a:a + n, :, 0:HD].bitcast(F32), ALU.subtract) \
                        .then_inc(s_vl, 1)

            def attention(b, units, table):
                starts = quad_starts(units)

                def mask(u):
                    i, h, k0, nkt = units[u]
                    dve.wait_ge(s_scored, b["scored"] + (u + 1))
                    if u >= 2:
                        dve.wait_ge(s_tp, b["tp"] + starts[u - 1])
                    dve.sem_inc(s_mask_may, 1)
                    ps = PS[:, 2 * (u % 2):2 * (u % 2) + 2, :].rearrange("p b n -> p (b n)")
                    nc.vector.tensor_tensor_reduce(PR[:, u % 2, 0:nkt * P], ps[:, 0:nkt * P],
                                                   table(i, h, nkt), -1.0, 3e38, ALU.add, ALU.min,
                                                   NM[:, u % 4:u % 4 + 1]).then_inc(s_masked, 1)

                def normalise(u):
                    i, h, k0, nkt = units[u]
                    dve.wait_ge(s_o_tmp, b["o_tmp"] + (u + 1))
                    if h == 0 and i >= 2:
                        dve.wait_ge(s_yt, b["yt"] + (i - 1))
                    nc.vector.scalar_tensor_tensor(YN[:, i % 2, h * HD:h * HD + HD],
                                                   PS[:, 6 + u % 2, 0:HD],
                                                   RC[:, u % 4:u % 4 + 1], OT[:, u % 2, :],
                                                   ALU.mult, ALU.add).then_inc(s_y, 1)

                mask(0)
                for u in range(NU + 1):
                    if u + 1 < NU:
                        mask(u + 1)
                    if u >= 1:
                        normalise(u - 1)
                    if u < NU:
                        for g, (a, n) in enumerate(quads(units[u][3])):
                            dve.wait_ge(s_pth, b["pth"] + (starts[u] + g + 1))
                            nc.vector.tensor_tensor(PTL[:, g, 0:n, :].rearrange("p t q -> p (t q)"),
                                                    PS[:, 4 + g, 0:n * P],
                                                    PTH[:, g, 0:n, :].rearrange("p t q -> p (t q)")
                                                    .bitcast(F32), ALU.subtract).then_inc(s_ptl, 1)
                        dve.wait_ge(s_exped, b["exped"] + (u + 1))
                        nc.vector.reciprocal(RC[:, u % 4:u % 4 + 1], SM[:, u % 4:u % 4 + 1]) \
                            .then_inc(s_recip, 1)

            def one_over(event, dst):
                dve.wait_ge(s_rooted, event + 1)
                n = dst.shape[1]
                nc.vector.reciprocal(dst, RT[:, 0:n]).then_inc(s_rstd, 1)

            def update_chunk(at, c, Y, t_y, which):
                t0, n = CHUNKS[c]
                one_over(at["rooted"] + 2 * c, R2[:, 0:n])
                dve.wait_ge(s_rstd, at["rstd"] + (2 * c + 1))

                def new_x(i):
                    z = Y[:, i, t_y:t_y + n]
                    nz = at["z"] + (24 * c + 3 * i)
                    nc.vector.scalar_tensor_tensor(z, z, GL[:, which * KT + i:which * KT + i + 1],
                                                   R2[:, 0:n], ALU.mult, ALU.mult).then_inc(s_z, 1)
                    dve.wait_ge(s_z, nz + 1)
                    nc.vector.tensor_tensor(z, z, XL[:, i, t0:t0 + n].bitcast(F32), ALU.add) \
                        .then_inc(s_z, 1)
                    dve.wait_ge(s_z, nz + 2)
                    nc.vector.tensor_tensor(z, z, XH[:, i, t0:t0 + n].bitcast(F32), ALU.add) \
                        .then_inc(s_z, 1)

                def low(i):
                    dve.wait_ge(s_xh, at["xh"] + (8 * c + i + 1))
                    nc.vector.tensor_tensor(XL[:, i, t0:t0 + n], Y[:, i, t_y:t_y + n],
                                            XH[:, i, t0:t0 + n].bitcast(F32), ALU.subtract) \
                        .then_inc(s_xl, 1)

                for i in range(KT + 1):
                    if i < KT:
                        new_x(i)
                    if i:
                        low(i - 1)
                one_over(at["rooted"] + (2 * c + 1), RS[:, t0:t0 + n])
                dve.wait_ge(s_xl, at["xl"] + 8 * (c + 1))
                dve.wait_ge(s_rstd, at["rstd"] + (2 * c + 2))

            nc.vector.memset(EPSC[:, :], EPS).then_inc(s_started, 1)
            dve.sem_inc(s_drained, 3)
            dve.sem_inc(s_cell, 1)
            dve.sem_inc(s_yout, 16)
            for c, (t0, n) in enumerate(CHUNKS):
                for i in range(KT):
                    dve.wait_ge(s_sq, 8 * c + i + 1)
                    nc.vector.tensor_tensor(XL[:, i, t0:t0 + n], PS[:, i % 6, 0:n],
                                            XH[:, i, t0:t0 + n].bitcast(F32), ALU.subtract) \
                        .then_inc(s_xl, 1)
                one_over(c, RS[:, t0:t0 + n])

            def dil_table(i, h, nkt):
                t = i if i < 8 else i - 8
                return TAB[:, 896 - P * t:896 - P * t + nkt * P]

            def na_table(i, h, nkt):
                if 2 <= i < 6:
                    return IB[:, h, :, :].rearrange("p r k -> p (r k)")
                t = i if i < 8 else i - 8
                e = 6 + 2 * (na_keys(i)[0] % 8 - t)
                return EB[:, h, e:e + 2 * nkt, :].rearrange("p r k -> p (r k)")

            with dve.Fori(0, DEPTH) as L:
                at = At(L)
                at.step("layer0")
                with dve.Fori(0, 3) as j:
                    b = at.body("dil", j)
                    dve.wait_ge(s_rstd, b["rstd"])
                    for block, (Z, factor) in enumerate(((TA, SCALE), (TB, 1.0), (TA, None))):
                        for c, (t0, n) in enumerate(CHUNKS):
                            scale_out(b, 3 * block + c, Z[:, t0:t0 + n], t0, n, c) \
                                .then_inc(s_drained, 1)
                        if block == 0:
                            rope(b, Z, 0, factor)
                            split_q(b)
                        if block == 1:
                            rope(b, Z, 1, factor)
                            split_k(b)
                    split_v(b)
                    attention(b, DIL_UNITS, dil_table)
                at.step("dil", 3)
                with dve.Fori(0, 2) as j:
                    b = at.body("na", j)
                    for block, (Z, factor) in enumerate(((TA, SCALE), (TB, None), (TA, None))):
                        for c, (t0, n) in enumerate(CHUNKS):
                            scale_out(b, 3 * block + c, Z[:, t0:t0 + n], t0, n, c, factor) \
                                .then_inc(s_drained, 1)
                        if block == 0:
                            split_q(b)
                        if block == 1:
                            split_k(b)
                    dve.wait_ge(s_bias_in, 16 * (b["bias_in"] + 4))
                    e3 = EB[:, :, :, :].rearrange("p h r k -> p (h r) k")
                    nc.vector.tensor_tensor(e3, e3, cmask.unsqueeze(1).to_broadcast([P, 28, GRID_W]),
                                            ALU.add).then_inc(s_cell, 1)
                    dve.wait_ge(s_cell, b["cell"] + 1)
                    nc.vector.tensor_copy(IB[:, :, :, :], EB[:, :, 2:12, :]).then_inc(s_cell, 1)
                    dve.wait_ge(s_cell, b["cell"] + 2)
                    nc.vector.memset(IB[0:64, :, 8:10, :], MASKED).then_inc(s_cell, 1)
                    nc.vector.memset(IB[64:128, :, 0:1, :], MASKED).then_inc(s_cell, 1)
                    nc.vector.memset(IB[64:128, :, 9:10, :], MASKED).then_inc(s_cell, 1)
                    dve.wait_ge(s_cell, b["cell"] + 5)
                    split_v(b)
                    attention(b, NA_UNITS, na_table)
                at.step("na", 2)
                with dve.Fori(0, 3) as j:
                    b = at.body("conv", j)
                    for block, Z in enumerate((TA, TB)):
                        for c, (t0, n) in enumerate(CHUNKS):
                            scale_out(b, 3 * block + c, Z[:, t0:t0 + n], t0, n, c) \
                                .then_inc(s_drained, 1)
                    for col in (0, S_SAMPLE + 1, T + 2):
                        nc.vector.memset(U[:, col:col + 1], 0.0).then_inc(s_cell, 1)
                    dve.wait_ge(s_drained, b["drained"] + 6)
                    for t0, n, o in ((0, S_SAMPLE, 1), (S_SAMPLE, S_PROMPT, S_SAMPLE + 2)):
                        nc.vector.tensor_tensor(U[:, o:o + n], TA[:, t0:t0 + n], TB[:, t0:t0 + n],
                                                ALU.mult).then_inc(s_cell, 1)
                    dve.wait_ge(s_cell, b["cell"] + 5)
                    dve.wait_ge(s_cw, 16 * (b["cw"] + 1))
                    w = T + 1
                    nc.vector.tensor_scalar(CV[:, 0:w], U[:, 1:1 + w], CW[:, 1:2], None, ALU.mult) \
                        .then_inc(s_cell, 1)
                    for n_cell, tap in ((6, 0), (7, 2)):
                        dve.wait_ge(s_cell, b["cell"] + n_cell)
                        nc.vector.scalar_tensor_tensor(CV[:, 0:w], U[:, tap:tap + w],
                                                       CW[:, tap:tap + 1], CV[:, 0:w], ALU.mult,
                                                       ALU.add).then_inc(s_cell, 1)
                    for c, (t0, n) in enumerate(CHUNKS):
                        scale_out(b, 6 + c, TA[:, t0:t0 + n], t0, n, c).then_inc(s_drained, 1)
                    dve.wait_ge(s_cell, b["cell"] + 8)
                    dve.wait_ge(s_drained, b["drained"] + 9)
                    dve.wait_ge(s_yout, 16 * b["yout"])
                    for t0, n, o in ((0, S_SAMPLE, 0), (S_SAMPLE, S_PROMPT, S_SAMPLE + 1)):
                        nc.vector.tensor_tensor(YB[:, t0:t0 + n], TA[:, t0:t0 + n], CV[:, o:o + n],
                                                ALU.mult).then_inc(s_yb, 1)
                at.step("conv", 3)
                for c, (t0, n) in enumerate(CHUNKS):
                    for i in range(KT):
                        dve.wait_ge(s_mhi, at["mhi"] + (8 * c + i + 1))
                        nc.vector.tensor_tensor(ML[:, i, 0:n], MS[:, i, 0:n],
                                                MH[:, i, 0:n].bitcast(F32), ALU.subtract) \
                            .then_inc(s_mlo, 1)
                    if c:
                        dve.wait_ge(s_sq, at["sq"] + 16 * c)
                    for nb in range(KT):
                        dve.wait_ge(s_group, at["group"] + (8 * c + nb + 1))
                        nc.vector.tensor_copy(Y2[:, nb, 0:n], PS[:, nb % 4, 0:n]) \
                            .then_inc(s_drained, 1)
                    update_chunk(at, c, Y2, 0, 1)
                at.step("out")

                def gate_out(at, g, i, c, bank, up_before):
                    t0, n = CHUNKS[c]
                    scale_out(at, g, SG[:, t0:t0 + n], t0, n, bank) \
                        .then_inc(s_gate, 1)
                    dve.wait_ge(s_gate, at["gate"] + (i + 1))
                    dve.sem_inc(s_drained, 1)

                def hidden_out(at, g, i, t, c, bank, sgr):
                    t0, n = CHUNKS[c]
                    dve.wait_ge(s_group, at["group"] + (g + 1))
                    dve.wait_ge(s_sgr, at["sgr"] + sgr)
                    if i >= 2:
                        dve.wait_ge(s_hl, at["hl"] + (i - 1))
                    nc.vector.tensor_tensor(HT[:, i % 2, 0:n], PS[:, bank, 0:n], SG[:, t0:t0 + n],
                                            ALU.mult).then_inc(s_h, 1)
                    dve.wait_ge(s_h, at["h"] + (i + 1))
                    dve.sem_inc(s_drained, 1)
                    dve.wait_ge(s_hh, at["hh"] + (i + 1))
                    nc.vector.tensor_tensor(HL[t][:, t0:t0 + n], HT[:, i % 2, 0:n],
                                            HH[t][:, t0:t0 + n].bitcast(F32), ALU.subtract) \
                        .then_inc(s_hl, 1)

                def down_out(at, g0, cleared):
                    for c, (t0, n) in enumerate(CHUNKS):
                        for nb in range(KT):
                            g = 8 * c + nb
                            dve.wait_ge(s_group, at["group"] + (g0 + g + 1))
                            if g == 0:
                                dve.wait_ge(s_cleared, cleared)
                            nc.vector.tensor_tensor(ACC[:, nb, t0:t0 + n], ACC[:, nb, t0:t0 + n],
                                                    PS[:, 6 + g % 2, 0:n], ALU.add) \
                                .then_inc(s_drained, 1)

                for c in range(NCH):
                    gate_out(at, c, c, c, c, None)
                at.step("ffn0")
                with dve.Fori(0, 10) as j:
                    b = at.body("ffn", j)
                    for c in range(NCH):
                        hidden_out(b, c, c, 0, c, 3 + c, c - 2)
                    for c in range(NCH):
                        gate_out(b, 3 + c, c, c, c, None)
                    for c in range(NCH):
                        hidden_out(b, 6 + c, 3 + c, 1, c, 3 + c, c + 1)
                    for c in range(NCH):
                        gate_out(b, 9 + c, 3 + c, c, c, None)
                    down_out(b, 12, at["cleared"] + 1)
                at.step("ffn", 10)
                for c in range(NCH):
                    hidden_out(at, c, c, 0, c, 3 + c, c - 2)
                for c in range(NCH):
                    gate_out(at, 3 + c, c, c, c, None)
                for c in range(NCH):
                    hidden_out(at, 6 + c, 3 + c, 1, c, 3 + c, c + 1)
                down_out(at, 9, at["cleared"] + 1)
                at.step("ffn1")
                for c, (t0, n) in enumerate(CHUNKS):
                    update_chunk(at, c, ACC, t0, 3)
                at.step("upd")

        @block.tensor
        def _(pe):
            def products(out, wh, wl, xh, xl, first, last):
                nc.tensor.matmul(out, wh, xh, start=first, stop=False)
                nc.tensor.matmul(out, wh, xl, start=False, stop=False)
                return nc.tensor.matmul(out, wl, xh, start=False, stop=last)

            def project(at, k, slot_w, g, banks, back, x_from=None, after=None):
                pe.wait_ge(s_lo, at["lo"] + (k + 1))
                for c, (t0, n) in enumerate(CHUNKS):
                    pe.wait_ge(s_drained, at["drained"] + (g + c - back + 1))
                    if x_from is not None:
                        pe.wait_ge(s_xl, x_from + 8 * (c + 1))
                    for t in range(KT):
                        last = products(PS[:, banks[c], 0:n], WH[slot_w][:, t, :],
                                        WL[slot_w][:, t, :], XH[:, t, t0:t0 + n],
                                        XL[:, t, t0:t0 + n], t == 0, t == KT - 1)
                    last.then_inc(s_group, 1)
                    if c == NCH - 1:
                        pe.wait_ge(s_group, at["group"] + (g + c + 1))
                        pe.sem_inc(s_used, 1)

            def sum_partitions(part, event, n):
                pe.wait_ge(s_part, part)
                pe.wait_ge(s_rooted, event)
                nc.tensor.matmul(PS[:, 7, 0:n], ones, SSA[:, 0:n], start=True, stop=True) \
                    .then_inc(s_sumd, 1)

            def update_chunk(at, c):
                n = CHUNKS[c][1]
                for e in (2 * c, 2 * c + 1):
                    sum_partitions(at["part"] + 8 * (e + 1), at["rooted"] + e, n)

            pe.sem_inc(s_used, 3)
            pe.wait_ge(s_consts, 16)
            pe.wait_ge(s_xin, 16 * TILES)
            for c, (t0, n) in enumerate(CHUNKS):
                for i in range(KT):
                    k = 8 * c + i
                    if i >= 6:
                        pe.wait_ge(s_xl, 8 * c + i - 5)
                        pe.wait_ge(s_sq, 8 * c + i - 5)
                    elif c:
                        pe.wait_ge(s_xl, 8 * c)
                        pe.wait_ge(s_sq, 8 * c)
                    for j in range(n // P):
                        last = nc.tensor.transpose(PS[:, i % 6, j * P:(j + 1) * P],
                                                   XIN[:, t0 // P + j, i * P:(i + 1) * P], ident)
                    last.then_inc(s_turned, 1)
                sum_partitions(8 * (c + 1), c, n)

            def turn_v(b):
                for g, (bank, a, n) in enumerate(VBANKS):
                    for j in range(n):
                        t = a + j
                        last = nc.tensor.transpose(PS[:, bank, j * P:(j + 1) * P],
                                                   TA[:, t * P:(t + 1) * P], ident)
                    last.then_inc(s_vt, 1)

            def attention(b, units):
                starts = quad_starts(units)

                def scores(u):
                    i, h, k0, nkt = units[u]
                    if u >= 2:
                        pe.wait_ge(s_masked, b["masked"] + (u - 1))
                    q = QS[h][:, i * P:(i + 1) * P]
                    for a, n in quads(nkt):
                        keys = slice((k0 + a) * P, (k0 + a + n) * P)
                        bank = PS[:, 2 * (u % 2) + a // 4, 0:n * P]
                        nc.tensor.matmul(bank, q, KH[h][:, keys], start=True, stop=False)
                        last = nc.tensor.matmul(bank, q, KL[h][:, keys], start=False, stop=True)
                    last.then_inc(s_scored, 1)

                def turn(u):
                    i, h, k0, nkt = units[u]
                    pe.wait_ge(s_exped, b["exped"] + (u + 1))
                    for g, (a, n) in enumerate(quads(nkt)):
                        for j in range(n):
                            last = nc.tensor.transpose(
                                PS[:, 4 + g, j * P:(j + 1) * P],
                                PR[:, u % 2, (a + j) * P:(a + j + 1) * P], ident)
                        last.then_inc(s_tp, 1)

                def values(u):
                    i, h, k0, nkt = units[u]
                    if u >= 2:
                        pe.wait_ge(s_y, b["y"] + (u - 1))
                    if u % 2 and u >= 3:
                        pe.wait_ge(s_yb, b["yb"] + (u - 1) // 2)
                    o = PS[:, 6 + u % 2, 0:P]
                    for g, (a, n) in enumerate(quads(nkt)):
                        pe.wait_ge(s_ptl, b["ptl"] + (starts[u] + g + 1))
                        for j in range(n):
                            v = V[:, k0 + a + j, h, :]
                            nc.tensor.matmul(o, PTH[:, g, j, :], v, start=a + j == 0, stop=False)
                            last = nc.tensor.matmul(o, PTL[:, g, j, :], v, start=False,
                                                    stop=a + j == nkt - 1)
                    last.then_inc(s_pv, 1)

                def turn_y(i):
                    pe.wait_ge(s_y, b["y"] + (2 * i + 2))
                    nc.tensor.transpose(PS[:, 7, 0:P], YN[:, i % 2, :],
                                        ident).then_inc(s_yt, 1)

                pe.wait_ge(s_stack_lo, b["stack_lo"] + 6)
                pe.wait_ge(s_drained, b["drained"] + 9)
                scores(0)
                scores(1)
                turn_v(b)
                pe.wait_ge(s_vl, b["vl"] + 3)
                for u in range(NU):
                    turn(u)
                    if u + 2 < NU:
                        scores(u + 2)
                    if u >= 2 and u % 2 == 0:
                        turn_y(u // 2 - 1)
                    values(u)
                turn_y(TILES - 1)

            with pe.Fori(0, DEPTH) as L:
                at = At(L)
                at.step("layer0")
                with pe.Fori(0, 3) as j:
                    b = at.body("dil", j)
                    for k in range(3):
                        project(b, k, k, 3 * k, (0, 1, 2), 3, at["xl"] - 24 if k == 0 else None)
                    attention(b, DIL_UNITS)
                at.step("dil", 3)
                with pe.Fori(0, 2) as j:
                    b = at.body("na", j)
                    for k in range(3):
                        project(b, k, k, 3 * k, (0, 1, 2), 3)
                    attention(b, NA_UNITS)
                at.step("na", 2)
                with pe.Fori(0, 3) as j:
                    b = at.body("conv", j)
                    for k in range(3):
                        project(b, k, k, 3 * k, (0, 1, 2), 3)
                at.step("conv", 3)
                for c, (t0, n) in enumerate(CHUNKS):
                    for nb in range(KT):
                        u = 8 * c + nb
                        pe.wait_ge(s_lo, at["lo"] + (u + 1))
                        pe.wait_ge(s_drained, at["drained"] + (u - 3 + 1))
                        for t in range(KT):
                            if nb == 0:
                                pe.wait_ge(s_mlo, at["mlo"] + (8 * c + t + 1))
                            last = products(PS[:, nb % 4, 0:n], WH[u % 3][:, t, :],
                                            WL[u % 3][:, t, :], MH[:, t, 0:n], ML[:, t, 0:n],
                                            t == 0, t == KT - 1)
                        last.then_inc(s_group, 1)
                        pe.wait_ge(s_group, at["group"] + (u + 1))
                        pe.sem_inc(s_used, 1)
                    update_chunk(at, c)
                at.step("out")

                def down(at, k, g0, hl):
                    pe.wait_ge(s_lo, at["lo"] + (k + 2))
                    for c, (t0, n) in enumerate(CHUNKS):
                        pe.wait_ge(s_hl, at["hl"] + (hl + c + 1))
                        for nb in range(KT):
                            g = 8 * c + nb
                            back = 2 if g >= 2 else 3
                            pe.wait_ge(s_drained, at["drained"] + (g0 + g - back + 1))
                            for t in range(2):
                                last = products(PS[:, 6 + g % 2, 0:n], WH[2 + t][:, nb, :],
                                                WL[2 + t][:, nb, :], HH[t][:, t0:t0 + n],
                                                HL[t][:, t0:t0 + n], t == 0, t == 1)
                            last.then_inc(s_group, 1)
                    pe.wait_ge(s_group, at["group"] + (g0 + 24))
                    pe.sem_inc(s_used, 1)
                    pe.sem_inc(s_used, 1)

                project(at, 0, 0, 0, (0, 1, 2), 3, at["xl"] - 24)
                at.step("ffn0")
                with pe.Fori(0, 10) as j:
                    b = at.body("ffn", j)
                    project(b, 0, 1, 0, (3, 4, 5), 3)
                    project(b, 1, 0, 3, (0, 1, 2), 3)
                    project(b, 2, 1, 6, (3, 4, 5), 3)
                    project(b, 3, 0, 9, (0, 1, 2), 3)
                    down(b, 4, 12, 3)
                at.step("ffn", 10)
                project(at, 0, 1, 0, (3, 4, 5), 3)
                project(at, 1, 0, 3, (0, 1, 2), 3)
                project(at, 2, 1, 6, (3, 4, 5), 3)
                down(at, 3, 9, 3)
                at.step("ffn1")
                pe.wait_ge(s_drained, at["drained"])
                for c in range(NCH):
                    update_chunk(at, c)
                at.step("upd")
            end = At(DEPTH)
            pe.wait_ge(s_xl, end["xl"])
            for i in range(TILES):
                for half in range(2):
                    k = 2 * i + half
                    if k >= 4:
                        pe.wait_ge(s_zo, k - 3)
                    for j in range(4):
                        last = nc.tensor.transpose(PS[:, k % 4, j * P:(j + 1) * P],
                                                   ACC[:, 4 * half + j, i * P:(i + 1) * P], ident)
                    last.then_inc(s_zt, 1)


VBANKS = ((4, 0, 4), (5, 4, 4), (7, 8, 2))


def quad_starts(units):
    starts = [0]
    for u in units:
        starts.append(starts[-1] + len(quads(u[3])))
    return starts


def kernel(x_prompt, x_sample, g_pre_mix, w_in, conv_w, rpb, w_out, g_post_mix,
           g_pre_ffn, w_gate, w_up, w_down, g_post_ffn):
    import concourse.bacc as bacc
    from concourse.bass_utils import run_bass_kernel_spmd

    nc = bacc.Bacc("TRN2", target_bir_lowering=False, num_devices=1, dynamic_dma_scratch_size=4096)
    x = np.concatenate([np.asarray(x_sample)[0], np.asarray(x_prompt)[0]], 0)
    gains = np.stack([np.asarray(g) for g in (g_pre_mix, g_post_mix, g_pre_ffn, g_post_ffn)], 1)
    gains = gains.reshape(DEPTH, 4, KT, P).transpose(0, 3, 1, 2).reshape(DEPTH, P, 4 * KT)
    taps = np.asarray(conv_w).reshape(DEPTH, 3, D_CONV // P, P).transpose(0, 2, 3, 1)
    padded = np.pad(np.asarray(rpb), ((0, 0), (0, 0), (0, 0), (48, 48)))
    windows = np.lib.stride_tricks.sliding_window_view(padded, GRID_W, axis=-1)[..., ::-1, :]
    windows = windows.transpose(0, 1, 3, 2, 4)
    tables, small = constants()
    arrays = {"x": x, "w_in": w_in, "w_out": w_out, "w_gate": w_gate, "w_up": w_up,
              "w_down": w_down, "gains": gains, "conv_w": taps, "rpb": windows,
              "tables": tables, "small": small}
    arrays = {k: np.ascontiguousarray(v) for k, v in arrays.items()}
    args = [nc.dram_tensor(k, v.shape, F32, kind="ExternalInput").ap() for k, v in arrays.items()]
    mixed = nc.dram_tensor("mixed", [KT, P, T], F32, kind="Internal").ap()
    out = nc.dram_tensor("out", [T, D], F32, kind="ExternalOutput").ap()
    build(nc, *args, mixed, out)
    r = run_bass_kernel_spmd(nc, [arrays], core_ids=[0])
    y = r.results[0]["out"]
    return y[S_SAMPLE:][None], y[:S_SAMPLE][None]
```

```python
from contextlib import ExitStack

import numpy as np

import concourse.bass as bass
from concourse import mybir

F32 = mybir.dt.float32
F32R = mybir.dt.float32r
ALU = mybir.AluOpType
ACT = mybir.ActivationFunctionType

P = 128
DEPTH = 2
D = 1024
KT = D // P
S_SAMPLE, S_PROMPT = 1024, 256
T = S_SAMPLE + S_PROMPT
CHUNKS = ((0, 512), (512, 512), (1024, 256))
NCH = len(CHUNKS)
TILES = T // P
HD = 64
D_DIL, D_NA, D_CONV = 384, 256, 384
D_IN = 3 * D
D_FF = 2816
FT = D_FF // P
GRID_W, NA_ROWS, NA_COLS = 64, 8, 16
EPS = 1e-6
SCRATCH = 256
MASKED = -1e30
SCALE = HD ** -0.5

DIL_UNITS = [(i, h, 0, 8) for i in range(8) for h in range(2)] + \
            [(i, h, 8, 2) for i in (8, 9) for h in range(2)]


def na_keys(i):
    if i >= 8:
        return 8, 2
    if i < 2:
        return 0, 4
    if i >= 6:
        return 4, 4
    return i - 2, 5


NA_UNITS = [(i, h) + na_keys(i) for i in range(TILES) for h in range(2)]


def quads(nkt):
    return [(a, min(4, nkt - a)) for a in range(0, nkt, 4)]


N_DQ = sum(len(quads(u[3])) for u in DIL_UNITS)
N_NQ = sum(len(quads(u[3])) for u in NA_UNITS)
NU = len(DIL_UNITS)

ATT = dict(scored=NU, masked=NU, exped=NU, pv=NU, o_tmp=NU, recip=NU, y=NU, yt=TILES, yb=TILES,
           yout=1, vt=3, vh=3, vl=3, stack_hi=6, stack_lo=6)
UPDATE = dict(sq=48, part=42, sumd=6, rooted=6, rstd=6, joined=24, z=48, xh=24, xl=24)
PER = {
    "layer0": dict(gains=1, tab=1),
    "dil": dict(trip=2, unit=6, gained=6, group=18, tp=N_DQ, pth=N_DQ, ptl=N_DQ, swap=8, cell=16,
                cw=1, cout=1, gated=2, convolved=2, **ATT),
    "na": dict(trip=1, unit=3, gained=3, group=9, tp=N_NQ, pth=N_NQ, ptl=N_NQ, cell=5, bias_in=4,
               **ATT),
    "out": dict(trip=8, unit=24, group=24, mload=3, mhi=24, mlo=24, **UPDATE),
    "ffn0": dict(unit=1, gained=1, group=3, gate=3, sig=3, sgr=3),
    "ffn": dict(trip=2, unit=6, gained=4, group=36, gate=6, sig=6, sgr=6, h=6, hh=6, hl=6),
    "ffn1": dict(unit=5, gained=3, group=33, gate=3, sig=3, sgr=3, h=6, hh=6, hl=6),
    "upd": dict(trip=2, cleared=1, **UPDATE),
}
COUNT = {"layer0": 1, "dil": 3, "na": 2, "out": 1, "ffn0": 1, "ffn": 10, "ffn1": 1, "upd": 1}
FIRST = dict(group=9, drained=3, lo=3, cell=1, yout=1, cout=1, sq=24, part=21, sumd=3, rooted=3,
             rstd=3, xh=24, xl=24)
SAME = {"hi": "unit", "lo": "unit", "drained": "group"}
ORDER = list(PER)

STEPS = ((), (0, 1), (2, 3), (4, 5), (6,), (7,), (8,), ())
ALL_STEPS = tuple(range(KT + 1))


def squares_out():
    order = []
    for c in range(NCH):
        for nb in range(KT):
            order.append(("y", c, nb))
            if c:
                order += [("x", c - 1, k) for k in STEPS[nb] if k < KT]
    return order + [("x", NCH - 1, k) for k in range(KT)]


def squares_upd():
    return [(kind, c, k) for kind, c in (("y", 0), ("y", 1), ("x", 0), ("y", 2), ("x", 1), ("x", 2))
            for k in range(KT)]


class Squares:

    def __init__(self, order):
        self.sq = {e: n for n, e in enumerate(order)}
        added = [e for e in order if e[2]]
        self.add = {e: n for n, e in enumerate(added)}

    def last_add(self, kind, c):
        return self.add[kind, c, KT - 1] + 1


SQ_OUT, SQ_UPD = Squares(squares_out()), Squares(squares_upd())
SQ_IN = Squares([("x", c, k) for c in range(NCH) for k in range(KT)])
EVENT = {("y", c): 2 * c for c in range(NCH)} | {("x", c): 2 * c + 1 for c in range(NCH)}
EVENT_IN = {("x", c): c for c in range(NCH)}
START = dict.fromkeys(("sq", "part", "sumd", "rooted", "rstd", "xh", "xl"), 0)


class At:

    def __init__(self, layer):
        self.base = {}
        self.names = {k for p in PER.values() for k in p} | set(SAME)
        for k in self.names:
            per = sum(PER[s].get(SAME.get(k, k), 0) * COUNT[s] for s in ORDER)
            self.base[k] = layer * per + FIRST.get(k, 0)

    def __getitem__(self, k):
        return self.base[k]

    def step(self, section, times=1):
        for k in self.names:
            self.base[k] = self.base[k] + times * PER[section].get(SAME.get(k, k), 0)

    def after(self, section, times=1):
        return self.body(section, times)

    def body(self, section, it):
        new = At.__new__(At)
        new.names = self.names
        new.base = {k: self.base[k] + it * PER[section].get(SAME.get(k, k), 0)
                    if PER[section].get(SAME.get(k, k), 0) else self.base[k] for k in self.names}
        return new


def constants():
    f = np.float32
    inv = (f(1.0) / (f(10000.0) ** (np.arange(0, HD, 2, dtype=f) / f(HD)))).astype(f)
    ang = (np.arange(S_SAMPLE, dtype=f)[None, :] * inv[:, None]).astype(f)
    cos, sin = np.cos(ang).astype(f), np.sin(ang).astype(f)
    cos128 = np.concatenate([cos] * 4, 0)
    sin128 = np.concatenate([-sin, sin, -sin, sin], 0)
    d = np.abs(np.arange(1920)[None, :] - 896 - np.arange(P)[:, None])
    count = (d <= 64).astype(int) + ((d % 4 == 0) & (d <= 256)) + (d % 16 == 0)
    log = np.where(count > 0, np.log(np.maximum(count, 1)), MASKED).astype(f)
    qc = np.arange(GRID_W)
    start = np.clip(qc - NA_COLS // 2, 0, GRID_W - NA_COLS)
    ok = (qc[None, :] >= start[:, None]) & (qc[None, :] < start[:, None] + NA_COLS)
    cmask = np.tile(np.where(ok, 0.0, MASKED).astype(f), (2, 1))
    eye_ones = np.concatenate([np.eye(P, dtype=f), np.ones((P, P), f), cmask], 1)
    return np.ascontiguousarray(np.concatenate([log, cos128, sin128], 1)), eye_ones


def build(nc, x, w_in, w_out, w_gate, w_up, w_down, gains, conv_w, rpb, tables, small, mixed, out):
    with ExitStack() as ctx:
        at = [SCRATCH]

        def place(name, shape, dt=F32, offset=None):
            size = int(np.prod(shape[1:])) * 4
            if offset is None:
                offset, at[0] = at[0], at[0] + (size + 31) // 32 * 32
            return nc.alloc_sbuf_tensor_at(name, shape, dt, offset=offset)

        XH = place("XH", [P, KT, T], F32R)
        XL = place("XL", [P, KT, T], F32R)
        X = place("X", [P, KT, T], offset=at[0] - KT * T * 4)
        RS = place("RS", [P, T])
        RAW = [place(f"RAW{s}", [P, KT, P]) for s in range(3)]
        WH, WL = [], []
        for s in range(4):
            WH.append(place(f"WH{s}", [P, KT, P], F32R))
            WL.append(place(f"WL{s}", [P, KT, P], F32R))
        w3 = at[0] - 8192
        EYE = place("EYE", [P, 2 * P + GRID_W])
        ident, ones, cmask = EYE[:, 0:P], EYE[:, P:2 * P], EYE[:, 2 * P:]
        GL = place("GL", [P, 4 * KT])
        CW = place("CW", [P, 3])
        EPSC = place("EPSC", [P, 1])
        base = at[0]
        STAT = place("STAT", [P, 12])
        NM = STAT[:, 0:4]
        SM = STAT[:, 4:8]
        RC = STAT[:, 8:12]
        OT = place("OT", [P, 2, HD])
        YN = place("YN", [P, 2, P])
        QS = [place(f"QS{h}", [P, T], F32R) for h in range(2)]
        KH = [place(f"KH{h}", [P, T], F32R) for h in range(2)]
        KL = [place(f"KL{h}", [P, T], F32R) for h in range(2)]
        TA = place("TA", [P, T + 4])
        TB = place("TB", [P, T + 4])
        TC = place("TC", [P, T + 4])
        V = place("V", [P, TILES, 2, P], F32R)
        PR = place("PR", [P, 2, 1024])
        YB = place("YB", [P, T])
        at[0] += 8192
        tab = at[0]
        TAB = place("TAB", [P, 1920 + 2 * 1024])
        assert at[0] <= 229247, at[0]
        EB = place("EB", [P, 2, 14, GRID_W], offset=tab)
        IB = place("IB", [P, 2, 10, GRID_W], offset=tab + 7168)
        PTH = [place("PTH0", [P, 2, 4, P], F32R, offset=w3),
               place("PTH1", [P, 2, 4, P], F32R, offset=tab - 8192)]
        PTL = [place("PTL0", [P, 2, 4, P], F32R, offset=w3 + 4096),
               place("PTL1", [P, 2, 4, P], F32R, offset=tab - 4096)]
        at[0] = base
        SQ = place("SQ", [P, 2, 512])
        SSY = place("SSY", [P, 512])
        SSX = place("SSX", [P, 512])
        SSUM = {"y": SSY, "x": SSX}
        RT = place("RT", [P, 512])
        past_norms = at[0]
        MS = place("MS", [P, KT, 512])
        MH = place("MH", [P, KT, 512], F32R)
        ML = place("ML", [P, KT, 512], F32R)
        YO = [place(f"YO{c}", [P, KT, 512]) for c in range(2)]
        assert at[0] <= 229247, at[0]
        at[0] = past_norms
        ACC = place("ACC", [P, KT, T])
        past_acc = at[0]
        HH = [place(f"HH{j}", [P, T], F32R) for j in range(2)]
        HL = [place(f"HL{j}", [P, T], F32R) for j in range(2)]
        SG = place("SG", [P, T])
        HT = place("HT", [P, 2, 512])
        assert at[0] <= 229247, at[0]
        ZO = place("ZO", [P, 2, D], offset=past_acc)
        XIN = place("XIN", [P, TILES, D], offset=past_norms)

        PS = ctx.enter_context(nc.psum_tensor("PS", [P, 8, 512], F32))

        def sem(name):
            return ctx.enter_context(nc.semaphore(name))

        s_consts = sem("consts")
        s_xin = sem("xin")
        s_turned = sem("turned")
        s_started = sem("started")
        s_gains = sem("gains")
        s_tab = sem("tab")
        s_bias_in = sem("bias_in")
        s_cw = sem("cw")
        s_load0 = sem("load0")
        s_load1 = sem("load1")
        s_load2 = sem("load2")
        s_gained = sem("gained")
        s_hi = sem("hi")
        s_lo = sem("lo")
        s_group = sem("group")
        s_drained = sem("drained")
        s_xh = sem("xh")
        s_xl = sem("xl")
        s_sq = sem("sq")
        s_part = sem("part")
        s_sumd = sem("sumd")
        s_rooted = sem("rooted")
        s_rstd = sem("rstd")
        s_joined = sem("joined")
        s_z = sem("z")
        s_cell = sem("cell")
        s_swap = sem("swap")
        s_stack_hi = sem("stack_hi")
        s_stack_lo = sem("stack_lo")
        s_mask_may = sem("mask_may")
        s_clear_may = sem("clear_may")
        s_vt = sem("vt")
        s_vh = sem("vh")
        s_vl = sem("vl")
        s_scored = sem("scored")
        s_masked = sem("masked")
        s_exped = sem("exped")
        s_tp = sem("tp")
        s_pth = sem("pth")
        s_ptl = sem("ptl")
        s_pv = sem("pv")
        s_o_tmp = sem("o_tmp")
        s_recip = sem("recip")
        s_y = sem("y")
        s_yt = sem("yt")
        s_yb = sem("yb")
        s_yout = sem("yout")
        s_mload = sem("mload")
        s_mhi = sem("mhi")
        s_mlo = sem("mlo")
        s_gate = sem("gate")
        s_sig = sem("sig")
        s_sgr = sem("sgr")
        s_h = sem("h")
        s_hh = sem("hh")
        s_hl = sem("hl")
        s_cleared = sem("cleared")
        s_gated = sem("gated")
        s_convolved = sem("convolved")
        s_cout = sem("cout")
        s_zt = sem("zt")
        s_zo = sem("zo")
        s_zout0 = sem("zout0")
        s_zout1 = sem("zout1")
        loads = (s_load0, s_load1, s_load2)
        zouts = (s_zout0, s_zout1)

        wv = {k: w.rearrange("l (t p) n -> l p t n", p=P)
              for k, w in (("in", w_in), ("out", w_out), ("gate", w_gate), ("up", w_up))}

        block = ctx.enter_context(nc.Block())

        @block.sync
        def _(sp):
            sp.dma_start(EYE[:, :], small).then_inc(s_consts, 16)
            for i in range(TILES):
                sp.dma_start(XIN[:, i, :], x[i * P:(i + 1) * P, :]).then_inc(s_xin, 16)

            def load(at, k, matrix, L, col, ring=0):
                slot = (ring + k) % 3
                sp.wait_ge(s_lo, at["lo"] + (k - 2))
                src = wv[matrix][bass.ds(L, 1), :, :, bass.ds(col, P)]
                sp.dma_start(RAW[slot][:, :, :], src.rearrange("l p t n -> (l p) t n")) \
                    .then_inc(loads[slot], 16)

            def load_down(at, k, L, row):
                slot = (1 + k) % 3
                sp.wait_ge(s_lo, at["lo"] + (k - 2))
                sp.dma_start(RAW[slot][:, :, :].rearrange("p t n -> p (t n)"),
                             w_down[bass.ds(L, 1), bass.ds(row, P), :]
                             .rearrange("l p n -> (l p) n")).then_inc(loads[slot], 16)

            with sp.Fori(0, DEPTH) as L:
                at = At(L)
                sp.wait_ge(s_xl, at["xl"])
                sp.dma_start(GL[:, :], gains[bass.ds(L, 1), :, :].rearrange("l p n -> (l p) n")) \
                    .then_inc(s_gains, 16)
                sp.dma_start(TAB[:, :], tables).then_inc(s_tab, 16)
                at.step("layer0")
                with sp.Fori(0, 3) as j:
                    b = at.body("dil", j)
                    for k in range(3):
                        load(b, k, "in", L, j * P + k * D_DIL)
                    sp.wait_ge(s_cell, b["cell"])
                    sp.dma_start(CW[:, :], conv_w[bass.ds(L, 1), bass.ds(j, 1), :, :]
                                 .rearrange("l c p w -> (l c p) w")).then_inc(s_cw, 16)
                    for k, part in enumerate((1, 2, 0)):
                        load(b, 3 + k, "in", L, j * P + (3 * D_DIL + 3 * D_NA + part * D_CONV))
                at.step("dil", 3)
                with sp.Fori(0, 2) as j:
                    b = at.body("na", j)
                    for k in range(3):
                        load(b, k, "in", L, j * P + 3 * D_DIL + k * D_NA)
                    sp.wait_ge(s_masked, b["masked"])
                    for half in range(2):
                        rows = slice(1, 15) if half == 0 else slice(0, 14)
                        for h in range(2):
                            sp.dma_start(
                                EB[64 * half:64 * half + 64, h, :, :],
                                rpb[bass.ds(L, 1), bass.ds(j * 2 + h, 1), :, rows, :]
                                .rearrange("l h q r k -> (l h q) r k")).then_inc(s_bias_in, 16)
                at.step("na", 2)
                for k in range(3):
                    load(at, k, "out", L, k * P)
                for c, (t0, n) in enumerate(CHUNKS):
                    if c == 0:
                        sp.wait_ge(s_yout, 16 * at["yout"])
                        sp.wait_ge(s_cout, 16 * at["cout"])
                    else:
                        sp.wait_ge(s_mlo, at["mlo"] + 8 * c)
                    sp.dma_start(MS[:, :, 0:n], mixed[:, :, t0:t0 + n].rearrange("b p n -> p b n")) \
                        .then_inc(s_mload, 16)
                    for u in range(8 * c + (3 if c == 0 else 0), 8 * c + 8):
                        load(at, u, "out", L, u % KT * P)
                at.step("out")
                load(at, 0, "gate", L, 0)
                at.step("ffn0")
                with sp.Fori(0, 10) as j:
                    b = at.body("ffn", j)
                    for k, (m, f) in enumerate((("up", 0), ("gate", 1), ("up", 1), ("gate", 2))):
                        load(b, k, m, L, j * (2 * P) + f * P, ring=1)
                    for k in range(2):
                        load_down(b, 4 + k, L, j * (2 * P) + k * P)
                at.step("ffn", 10)
                for k, (m, f) in enumerate((("up", 20), ("gate", 21), ("up", 21))):
                    load(at, k, m, L, f * P, ring=1)
                for k in range(2):
                    load_down(at, 3 + k, L, (20 + k) * P)
                at.step("ffn1")
                at.step("upd")
            for i in range(TILES):
                sp.wait_ge(s_zo, 2 * i + 2)
                sp.dma_start(out[i * P:(i + 1) * P, :], ZO[:, i % 2, :]).then_inc(zouts[i % 2], 16)
            for half in range(2):
                sp.wait_ge(zouts[half], 16 * (TILES // 2))

        @block.gpsimd
        def _(pool):
            def gain(at, k, g, which, ring=0):
                slot = (ring + k) % 3
                pool.wait_ge(loads[slot], 16 * (at["trip"] + ((ring + k) // 3 + 1)))
                gcol = GL[:, which * KT:which * KT + KT].unsqueeze(2).to_broadcast([P, KT, P])
                nc.gpsimd.tensor_tensor(RAW[slot][:, :, :], RAW[slot][:, :, :], gcol, ALU.mult) \
                    .then_inc(s_gained, 1)

            def low(at, k, slot_w, ring=0):
                slot = (ring + k) % 3
                pool.wait_ge(s_hi, at["hi"] + (k + 1))
                nc.gpsimd.tensor_tensor(WL[slot_w][:, :, :], RAW[slot][:, :, :],
                                        WH[slot_w][:, :, :].bitcast(F32), ALU.subtract) \
                    .then_inc(s_lo, 1)

            def add_square(at, order, event, kind, c, i):
                if i == 0:
                    return
                n = CHUNKS[c][1]
                k = order.add[kind, c, i]
                pool.wait_ge(s_sq, at["sq"] + (order.sq[kind, c, i] + 1))
                if i > 1:
                    pool.wait_ge(s_part, at["part"] + (order.add[kind, c, i - 1] + 1))
                nc.gpsimd.tensor_tensor(SSUM[kind][:, 0:n], SSUM[kind][:, 0:n], SQ[:, k % 2, 0:n],
                                        ALU.add).then_inc(s_part, 1)

            def join(c, used):
                t0, n = CHUNKS[c]
                for k in range(KT):
                    pool.wait_ge(s_group, used)
                    nc.gpsimd.tensor_tensor(X[:, k, t0:t0 + n],
                                            XL[:, k, t0:t0 + n].bitcast(F32),
                                            XH[:, k, t0:t0 + n].bitcast(F32), ALU.add) \
                        .then_inc(s_joined, 1)

            pool.sem_inc(s_lo, 3)
            for kind, c, i in SQ_IN.sq:
                add_square(START, SQ_IN, EVENT_IN, kind, c, i)
            with pool.Fori(0, DEPTH) as L:
                at = At(L)
                at.step("layer0")
                with pool.Fori(0, 3) as j:
                    b = at.body("dil", j)
                    pool.wait_ge(s_gains, 16 * b["gains"])
                    for k in range(6):
                        gain(b, k, k, 0)
                        low(b, k, k % 3)
                    for k, (t0, n, o) in enumerate(CONV_PARTS):
                        pool.wait_ge(s_drained, b["drained"] + 15)
                        pool.wait_ge(s_cell, b["cell"] + 13)
                        nc.gpsimd.tensor_tensor(TC[:, o:o + n], TA[:, t0:t0 + n], TB[:, t0:t0 + n],
                                                ALU.mult).then_inc(s_gated, 1)
                    for t0, n, o in CONV_PARTS:
                        pool.wait_ge(s_drained, b["drained"] + 18)
                        pool.wait_ge(s_cell, b["cell"] + 16)
                        nc.gpsimd.tensor_tensor(TB[:, t0:t0 + n], TB[:, t0:t0 + n],
                                                TA[:, o - 1:o - 1 + n], ALU.mult) \
                            .then_inc(s_convolved, 1)
                at.step("dil", 3)
                with pool.Fori(0, 2) as j:
                    b = at.body("na", j)
                    for k in range(3):
                        gain(b, k, k, 0)
                        low(b, k, k)
                at.step("na", 2)
                ffn = at.after("out")
                for c in range(NCH):
                    join(c, at["group"])

                def unit_low(u):
                    if u < 24:
                        low(at, u, u % 3)
                    if u == 24:
                        gain(ffn, 0, 0, 2)
                        low(ffn, 0, 0)

                for u in range(3):
                    unit_low(u)
                for c in range(NCH):
                    for nb in range(KT):
                        add_square(at, SQ_OUT, EVENT, "y", c, nb)
                        unit_low(8 * c + nb + 3)
                        for k in STEPS[nb] if c else ():
                            if k < KT:
                                add_square(at, SQ_OUT, EVENT, "x", c - 1, k)
                for k in range(KT):
                    add_square(at, SQ_OUT, EVENT, "x", NCH - 1, k)
                at.step("out")

                def scaled_gate(at, i, c):
                    t0, n = CHUNKS[c]
                    pool.wait_ge(s_sig, at["sig"] + (i + 1))
                    nc.gpsimd.tensor_tensor(SG[:, t0:t0 + n], SG[:, t0:t0 + n], RS[:, t0:t0 + n],
                                            ALU.mult).then_inc(s_sgr, 1)

                pool.wait_ge(s_xl, at["xl"])
                pool.sem_inc(s_clear_may, 1)
                nc.gpsimd.memset(ACC[:, :, :], 0.0).then_inc(s_cleared, 1)
                for c in range(NCH):
                    scaled_gate(at, c, c)
                at.step("ffn0")
                with pool.Fori(0, 10) as j:
                    b = at.body("ffn", j)
                    for k, w in ((0, 1), (1, 0), (2, 1)):
                        gain(b, k, k, 2, ring=1)
                        low(b, k, w, ring=1)
                    for c in range(NCH):
                        scaled_gate(b, c, c)
                    gain(b, 3, 3, 2, ring=1)
                    low(b, 3, 0, ring=1)
                    low(b, 4, 2, ring=1)
                    low(b, 5, 3, ring=1)
                    for c in range(NCH):
                        scaled_gate(b, 3 + c, c)
                at.step("ffn", 10)
                for k, w in ((0, 1), (1, 0), (2, 1)):
                    gain(at, k, k, 2, ring=1)
                    low(at, k, w, ring=1)
                for c in range(NCH):
                    scaled_gate(at, c, c)
                low(at, 3, 2, ring=1)
                low(at, 4, 3, ring=1)
                for c in range(NCH):
                    join(c, at["group"] + 9)
                at.step("ffn1")
                for kind, c, i in SQ_UPD.sq:
                    add_square(at, SQ_UPD, EVENT, kind, c, i)
                at.step("upd")

        @block.scalar
        def _(act):
            def high(at, k, slot_w, free, gained=None, ring=0):
                slot = (ring + k) % 3
                if gained is None:
                    act.wait_ge(loads[slot], 16 * (at["trip"] + ((ring + k) // 3 + 1)))
                else:
                    act.wait_ge(s_gained, at["gained"] + (gained + 1))
                act.wait_ge(s_group, at["group"] + free)
                nc.scalar.activation(WH[slot_w][:, :, :], RAW[slot][:, :, :], ACT.Copy) \
                    .then_inc(s_hi, 1)

            def square(at, order, event, src, kind, c, i):
                n = CHUNKS[c][1]
                if i == 0:
                    if (kind, c - 1) in event:
                        act.wait_ge(s_sumd, at["sumd"] + (event[kind, c - 1] + 1))
                    elif at is not START:
                        act.wait_ge(s_sumd, at["sumd"])
                    dst = SSUM[kind][:, 0:n]
                else:
                    k = order.add[kind, c, i]
                    if k >= 2:
                        act.wait_ge(s_part, at["part"] + (k - 1))
                    elif at is not START:
                        act.wait_ge(s_part, at["part"])
                    dst = SQ[:, k % 2, 0:n]
                nc.scalar.activation(dst, src, ACT.Square).then_inc(s_sq, 1)

            def root(at, event, n):
                act.wait_ge(s_sumd, at["sumd"] + (event + 1))
                if event or at is not START:
                    act.wait_ge(s_rstd, at["rstd"] + event)
                nc.scalar.activation(RT[:, 0:n], PS[:, SUM_BANK, 0:n], ACT.Sqrt, scale=1.0 / D,
                                     bias=EPSC[:, 0:1]).then_inc(s_rooted, 1)

            def new_high(at, order, Y, t_y, c, i):
                t0, n = CHUNKS[c]
                act.wait_ge(s_z, at["z"] + 16 * c + 2 * (i + 1))
                nc.scalar.activation(XH[:, i, t0:t0 + n], Y[:, i, t_y:t_y + n], ACT.Copy) \
                    .then_inc(s_xh, 1)
                square(at, order, EVENT, Y[:, i, t_y:t_y + n], "x", c, i)

            act.wait_ge(s_started, 1)
            for c, (t0, n) in enumerate(CHUNKS):
                for i in range(KT):
                    act.wait_ge(s_turned, 8 * c + i + 1)
                    nc.scalar.activation(XH[:, i, t0:t0 + n], PS[:, i % 4, 0:n], ACT.Copy) \
                        .then_inc(s_xh, 1)
                    square(START, SQ_IN, EVENT_IN, PS[:, i % 4, 0:n], "x", c, i)
                root(START, c, n)

            def split_q(b, src_ready):
                src_ready()
                nc.scalar.activation(QS[0][0:64, :], TA[0:64, 0:T], ACT.Copy).then_inc(s_stack_hi, 1)
                nc.scalar.activation(QS[1][64:128, :], TA[64:128, 0:T], ACT.Copy) \
                    .then_inc(s_stack_hi, 1)

            def split_k(b, src_ready):
                src_ready()
                for h in range(2):
                    own = TB[64 * h:64 * h + 64, 0:T]
                    for half in (h, 1 - h):
                        nc.scalar.activation(KH[h][64 * half:64 * half + 64, :], own, ACT.Copy) \
                            .then_inc(s_stack_hi, 1)

            def swap_halves(b, src, group, cell):
                act.wait_ge(s_drained, b["drained"] + group)
                act.wait_ge(s_cell, b["cell"] + cell)
                for q in range(4):
                    o = q ^ 1
                    nc.scalar.activation(TC[32 * o:32 * o + 32, 0:T], src[32 * q:32 * q + 32, 0:T],
                                         ACT.Copy).then_inc(s_swap, 1)

            def split_v(b):
                for g, (bank, a, n) in enumerate(VBANKS):
                    act.wait_ge(s_vt, b["vt"] + (g + 1))
                    ps = PS[:, bank, 0:n * P].rearrange("p (t h d) -> p t h d", h=2, d=HD)
                    nc.scalar.activation(V[:, a:a + n, :, 0:HD], ps, ACT.Copy).then_inc(s_vh, 1)

            def attention(b, units, banks):
                starts = quad_starts(units)

                def exp(u):
                    i, h, k0, nkt = units[u]
                    act.wait_ge(s_masked, b["masked"] + (u + 1))
                    nc.scalar.activation(PR[:, u % 2, 0:nkt * P], PR[:, u % 2, 0:nkt * P], ACT.Exp,
                                         scale=-1.0, bias=NM[:, u % 4:u % 4 + 1],
                                         accum_out=SM[:, u % 4:u % 4 + 1]).then_inc(s_exped, 1)

                def o_low(u):
                    act.wait_ge(s_pv, b["pv"] + (u + 1))
                    act.wait_ge(s_recip, b["recip"] + (u + 1))
                    if u >= 2:
                        act.wait_ge(s_y, b["y"] + (u - 1))
                    nc.scalar.activation(OT[:, u % 2, :], PS[:, banks[u % 2], HD:P],
                                         ACT.Copy, scale=RC[:, u % 4:u % 4 + 1]) \
                        .then_inc(s_o_tmp, 1)

                def y_block(i):
                    act.wait_ge(s_yt, b["yt"] + (i + 1))
                    if i == 0:
                        act.wait_ge(s_yout, 16 * b["yout"])
                    nc.scalar.activation(YB[:, i * P:(i + 1) * P],
                                         PS[:, banks[1], 0:P], ACT.Copy) \
                        .then_inc(s_yb, 1)

                exp(0)
                for u in range(NU + 2):
                    if u < NU:
                        for g, (a, n) in enumerate(quads(units[u][3])):
                            act.wait_ge(s_tp, b["tp"] + (starts[u] + g + 1))
                            if u >= 2:
                                act.wait_ge(s_pv, b["pv"] + (u - 1))
                            nc.scalar.activation(
                                PTH[u % 2][:, g, 0:n, :].rearrange("p t q -> p (t q)"),
                                PS[:, 4 + g, 0:n * P], ACT.Copy).then_inc(s_pth, 1)
                    if u >= 3 and u % 2:
                        y_block(u // 2 - 1)
                    if u + 1 < NU:
                        exp(u + 1)
                    if 1 <= u <= NU:
                        o_low(u - 1)

            def store_block(b, block):
                act.wait_ge(s_yb, b["yb"] + TILES)
                act.dma_start(mixed[bass.ds(block, 1), :, :].rearrange("b p n -> (b p) n"),
                              YB[:, :]).then_inc(s_yout, 16)

            with act.Fori(0, DEPTH) as L:
                at = At(L)
                at.step("layer0")
                with act.Fori(0, 3) as j:
                    b = at.body("dil", j)
                    for k in range(3):
                        high(b, k, k, 3 * k - 6, gained=k)
                    swap_halves(b, TA, 3, 0)
                    split_q(b, lambda: act.wait_ge(s_cell, b["cell"] + 5))
                    swap_halves(b, TB, 6, 5)
                    split_k(b, lambda: act.wait_ge(s_cell, b["cell"] + 10))
                    high(b, 3, 0, 3, gained=3)
                    split_v(b)
                    high(b, 4, 1, 6, gained=4)
                    high(b, 5, 2, 9, gained=5)
                    attention(b, DIL_UNITS, DIL_OUT)
                    store_block(b, j)
                    act.wait_ge(s_convolved, b["convolved"] + 2)
                    act.dma_start(mixed[bass.ds(j + 5, 1), :, :].rearrange("b p n -> (b p) n"),
                                  TB[:, 0:T]).then_inc(s_cout, 16)
                at.step("dil", 3)
                with act.Fori(0, 2) as j:
                    b = at.body("na", j)
                    for k in range(3):
                        high(b, k, k, 3 * k - 6, gained=k)
                    split_q(b, lambda: act.wait_ge(s_drained, b["drained"] + 3))
                    split_k(b, lambda: act.wait_ge(s_drained, b["drained"] + 6))
                    split_v(b)
                    attention(b, NA_UNITS, NA_OUT)
                    store_block(b, j + 3)
                at.step("na", 2)
                ffn = at.after("out")

                def unit_high(u):
                    if u < 24:
                        high(at, u, u % 3, u - 2 if u >= 3 else 3 * u - 6)
                    if u == 24:
                        high(ffn, 0, 0, -2, gained=0)

                def mixed_high(c):
                    t0, n = CHUNKS[c]
                    act.wait_ge(s_mload, 16 * (at["mload"] + (c + 1)))
                    act.wait_ge(s_group, at["group"] + 8 * c)
                    for i in range(KT):
                        nc.scalar.activation(MH[:, i, 0:n], MS[:, i, 0:n], ACT.Copy) \
                            .then_inc(s_mhi, 1)

                mixed_high(0)
                for u in range(3):
                    unit_high(u)
                for c, (t0, n) in enumerate(CHUNKS):
                    for nb in range(KT):
                        act.wait_ge(s_drained, at["drained"] + (8 * c + nb + 1))
                        square(at, SQ_OUT, EVENT, YO[c % 2][:, nb, 0:n], "y", c, nb)
                        if nb == KT - 1 and c + 1 < NCH:
                            mixed_high(c + 1)
                        unit_high(8 * c + nb + 3)
                        if c and nb == 0:
                            root(at, EVENT["y", c - 1], CHUNKS[c - 1][1])
                        for k in STEPS[nb] if c else ():
                            if k < KT:
                                new_high(at, SQ_OUT, YO[(c - 1) % 2], 0, c - 1, k)
                    if c:
                        root(at, EVENT["x", c - 1], CHUNKS[c - 1][1])
                root(at, EVENT["y", 2], CHUNKS[2][1])
                for k in range(KT):
                    new_high(at, SQ_OUT, YO[0], 0, 2, k)
                root(at, EVENT["x", 2], CHUNKS[2][1])
                at.step("out")

                def silu(at, i, c):
                    t0, n = CHUNKS[c]
                    act.wait_ge(s_gate, at["gate"] + (i + 1))
                    nc.scalar.activation(SG[:, t0:t0 + n], SG[:, t0:t0 + n], ACT.Silu) \
                        .then_inc(s_sig, 1)

                def hidden_high(at, i, t, c):
                    t0, n = CHUNKS[c]
                    act.wait_ge(s_h, at["h"] + (i + 1))
                    nc.scalar.activation(HH[t][:, t0:t0 + n], HT[:, i % 2, 0:n], ACT.Copy) \
                        .then_inc(s_hh, 1)

                for c in range(NCH):
                    silu(at, c, c)
                at.step("ffn0")
                with act.Fori(0, 10) as j:
                    b = at.body("ffn", j)
                    high(b, 0, 1, -27, gained=0, ring=1)
                    high(b, 1, 0, -24, gained=1, ring=1)
                    for c in range(NCH):
                        hidden_high(b, c, 0, c)
                    high(b, 2, 1, 3, gained=2, ring=1)
                    for c in range(NCH):
                        silu(b, c, c)
                    high(b, 3, 0, 6, gained=3, ring=1)
                    high(b, 4, 2, 0, ring=1)
                    high(b, 5, 3, 0, ring=1)
                    for c in range(NCH):
                        hidden_high(b, 3 + c, 1, c)
                    for c in range(NCH):
                        silu(b, 3 + c, c)
                at.step("ffn", 10)
                high(at, 0, 1, -27, gained=0, ring=1)
                high(at, 1, 0, -24, gained=1, ring=1)
                for c in range(NCH):
                    hidden_high(at, c, 0, c)
                high(at, 2, 1, 3, gained=2, ring=1)
                for c in range(NCH):
                    silu(at, c, c)
                high(at, 3, 2, 0, ring=1)
                high(at, 4, 3, 0, ring=1)
                for c in range(NCH):
                    hidden_high(at, 3 + c, 1, c)
                at.step("ffn1")
                for kind, c, i in SQ_UPD.sq:
                    t0, n = CHUNKS[c]
                    if kind == "x" and i == 0:
                        root(at, EVENT["y", c], n)
                    if kind == "x":
                        new_high(at, SQ_UPD, ACC, t0, c, i)
                        if i == KT - 1:
                            root(at, EVENT["x", c], n)
                    else:
                        act.wait_ge(s_drained, at["drained"] + (8 * c + i + 1 - 24))
                        square(at, SQ_UPD, EVENT, ACC[:, i, t0:t0 + n], "y", c, i)
                at.step("upd")
            for i in range(TILES):
                act.wait_ge(s_zt, 2 * i + 2)
                if i >= 2:
                    act.wait_ge(zouts[i % 2], 16 * (i // 2))
                nc.scalar.activation(ZO[:, i % 2, 0:512], PS[:, (2 * i) % 4, :], ACT.Copy) \
                    .then_inc(s_zo, 1)
                nc.scalar.activation(ZO[:, i % 2, 512:1024], PS[:, (2 * i + 1) % 4, :], ACT.Copy) \
                    .then_inc(s_zo, 1)

        @block.vector
        def _(dve):
            def scale_out(b, g, dst, t0, n, bank, factor=None):
                dve.wait_ge(s_group, b["group"] + (g + 1))
                if factor is None:
                    ins = nc.vector.tensor_tensor(dst, PS[:, bank, 0:n], RS[:, t0:t0 + n], ALU.mult)
                else:
                    ins = nc.vector.scalar_tensor_tensor(dst, PS[:, bank, 0:n], factor,
                                                         RS[:, t0:t0 + n], ALU.mult, ALU.mult)
                return ins

            def rope(b, X, block, factor):
                dve.wait_ge(s_tab, 16 * (b["tab"]))
                dve.wait_ge(s_swap, b["swap"] + 4 * (block + 1))
                dve.wait_ge(s_drained, b["drained"] + 3 * (block + 1))
                for Z, col in ((X, 1920), (TC, 1920 + 1024)):
                    for t0, n in ((0, S_SAMPLE), (S_SAMPLE, S_PROMPT)):
                        nc.vector.scalar_tensor_tensor(Z[:, t0:t0 + n], Z[:, t0:t0 + n], factor,
                                                       TAB[:, col:col + n], ALU.mult, ALU.mult) \
                            .then_inc(s_cell, 1)
                dve.wait_ge(s_cell, b["cell"] + (5 * block + 4))
                nc.vector.tensor_tensor(X[:, 0:T], X[:, 0:T], TC[:, 0:T], ALU.add).then_inc(s_cell, 1)

            def split_q(b):
                dve.wait_ge(s_stack_hi, b["stack_hi"] + 2)
                nc.vector.tensor_tensor(QS[0][64:128, :], TA[0:64, 0:T], QS[0][0:64, :].bitcast(F32),
                                        ALU.subtract).then_inc(s_stack_lo, 1)
                nc.vector.tensor_tensor(QS[1][0:64, :], TA[64:128, 0:T],
                                        QS[1][64:128, :].bitcast(F32), ALU.subtract) \
                    .then_inc(s_stack_lo, 1)

            def split_k(b):
                for h in range(2):
                    own = slice(64 * h, 64 * h + 64)
                    dve.wait_ge(s_stack_hi, b["stack_hi"] + 4 + 2 * h)
                    for half in (h, 1 - h):
                        nc.vector.tensor_tensor(KL[h][64 * half:64 * half + 64, :], TB[own, 0:T],
                                                KH[h][own, :].bitcast(F32), ALU.subtract) \
                            .then_inc(s_stack_lo, 1)

            def split_v(b):
                for g, (bank, a, n) in enumerate(VBANKS):
                    dve.wait_ge(s_vh, b["vh"] + (g + 1))
                    ps = PS[:, bank, 0:n * P].rearrange("p (t h d) -> p t h d", h=2, d=HD)
                    nc.vector.tensor_tensor(V[:, a:a + n, :, HD:P], ps,
                                            V[:, a:a + n, :, 0:HD].bitcast(F32), ALU.subtract) \
                        .then_inc(s_vl, 1)

            def attention(b, units, banks, table, beside=None):
                starts = quad_starts(units)

                def mask(u):
                    i, h, k0, nkt = units[u]
                    dve.wait_ge(s_scored, b["scored"] + (u + 1))
                    if u >= 2:
                        dve.wait_ge(s_tp, b["tp"] + starts[u - 1])
                    dve.sem_inc(s_mask_may, 1)
                    ps = PS[:, 2 * (u % 2):2 * (u % 2) + 2, :].rearrange("p b n -> p (b n)")
                    nc.vector.tensor_tensor_reduce(PR[:, u % 2, 0:nkt * P], ps[:, 0:nkt * P],
                                                   table(i, h, nkt), -1.0, 3e38, ALU.add, ALU.min,
                                                   NM[:, u % 4:u % 4 + 1]).then_inc(s_masked, 1)

                def normalise(u):
                    i, h, k0, nkt = units[u]
                    dve.wait_ge(s_o_tmp, b["o_tmp"] + (u + 1))
                    if h == 0 and i >= 2:
                        dve.wait_ge(s_yt, b["yt"] + (i - 1))
                    nc.vector.scalar_tensor_tensor(YN[:, i % 2, h * HD:h * HD + HD],
                                                   PS[:, banks[u % 2], 0:HD],
                                                   RC[:, u % 4:u % 4 + 1], OT[:, u % 2, :],
                                                   ALU.mult, ALU.add).then_inc(s_y, 1)

                mask(0)
                mask(1)
                for u in range(NU + 1):
                    if beside is not None:
                        beside(u)
                    if u < NU:
                        for g, (a, n) in enumerate(quads(units[u][3])):
                            dve.wait_ge(s_pth, b["pth"] + (starts[u] + g + 1))
                            high = PTH[u % 2][:, g, 0:n, :].rearrange("p t q -> p (t q)")
                            nc.vector.tensor_tensor(
                                PTL[u % 2][:, g, 0:n, :].rearrange("p t q -> p (t q)"),
                                PS[:, 4 + g, 0:n * P], high.bitcast(F32), ALU.subtract) \
                                .then_inc(s_ptl, 1)
                    if u + 2 < NU:
                        mask(u + 2)
                    if u < NU:
                        dve.wait_ge(s_exped, b["exped"] + (u + 1))
                        nc.vector.reciprocal(RC[:, u % 4:u % 4 + 1], SM[:, u % 4:u % 4 + 1]) \
                            .then_inc(s_recip, 1)
                    if u >= 1:
                        normalise(u - 1)

            def one_over(at, event, dst):
                dve.wait_ge(s_rooted, at["rooted"] + (event + 1))
                nc.vector.reciprocal(dst, RT[:, 0:dst.shape[1]]).then_inc(s_rstd, 1)

            def step(at, Y, t_y, c, k, which):
                t0, n = CHUNKS[c]
                if k == 0:
                    dve.wait_ge(s_rstd, at["rstd"] + (EVENT["y", c] + 1))
                if k < KT:
                    z = Y[:, k, t_y:t_y + n]
                    nz = at["z"] + (16 * c + 2 * k)
                    nc.vector.scalar_tensor_tensor(z, z, GL[:, which * KT + k:which * KT + k + 1],
                                                   RT[:, 0:n], ALU.mult, ALU.mult).then_inc(s_z, 1)
                    dve.wait_ge(s_joined, at["joined"] + (8 * c + k + 1))
                    dve.wait_ge(s_z, nz + 1)
                    nc.vector.tensor_tensor(z, z, X[:, k, t0:t0 + n], ALU.add) \
                        .then_inc(s_z, 1)
                if k:
                    i = k - 1
                    dve.wait_ge(s_xh, at["xh"] + (8 * c + i + 1))
                    nc.vector.tensor_tensor(XL[:, i, t0:t0 + n], Y[:, i, t_y:t_y + n],
                                            XH[:, i, t0:t0 + n].bitcast(F32), ALU.subtract) \
                        .then_inc(s_xl, 1)

            nc.vector.memset(EPSC[:, :], EPS).then_inc(s_started, 1)
            dve.sem_inc(s_drained, 3)
            dve.sem_inc(s_cell, 1)
            dve.sem_inc(s_yout, 16)
            dve.sem_inc(s_cout, 16)
            for c, (t0, n) in enumerate(CHUNKS):
                for i in range(KT):
                    dve.wait_ge(s_sq, 8 * c + i + 1)
                    nc.vector.tensor_tensor(XL[:, i, t0:t0 + n], PS[:, i % 4, 0:n],
                                            XH[:, i, t0:t0 + n].bitcast(F32), ALU.subtract) \
                        .then_inc(s_xl, 1)
                one_over(START, c, RS[:, t0:t0 + n])

            def dil_table(i, h, nkt):
                t = i if i < 8 else i - 8
                return TAB[:, 896 - P * t:896 - P * t + nkt * P]

            def na_table(i, h, nkt):
                if 2 <= i < 6:
                    return IB[:, h, :, :].rearrange("p r k -> p (r k)")
                t = i if i < 8 else i - 8
                e = 6 + 2 * (na_keys(i)[0] % 8 - t)
                return EB[:, h, e:e + 2 * nkt, :].rearrange("p r k -> p (r k)")

            with dve.Fori(0, DEPTH) as L:
                at = At(L)
                at.step("layer0")
                with dve.Fori(0, 3) as j:
                    b = at.body("dil", j)
                    dve.wait_ge(s_rstd, b["rstd"])
                    for block, (Z, factor) in enumerate(((TA, SCALE), (TB, 1.0), (TA, None))):
                        if block == 0:
                            dve.wait_ge(s_convolved, b["convolved"])
                        if block == 1:
                            dve.wait_ge(s_cout, 16 * b["cout"])
                        for c, (t0, n) in enumerate(CHUNKS):
                            scale_out(b, 3 * block + c, Z[:, t0:t0 + n], t0, n, c) \
                                .then_inc(s_drained, 1)
                        if block == 0:
                            rope(b, Z, 0, factor)
                            split_q(b)
                        if block == 1:
                            rope(b, Z, 1, factor)
                            split_k(b)
                    split_v(b)

                    def convolution(u):
                        if 2 <= u < 20 and u % 2 == 0:
                            g = u // 2 - 1
                            t0, n = CHUNKS[g % 3]
                            Z = (TA, TB, TB)[g // 3]
                            if g == 6:
                                dve.wait_ge(s_gated, b["gated"] + 2)
                            scale_out(b, 9 + g, Z[:, t0:t0 + n], t0, n, 7).then_inc(s_drained, 1)
                        if u == 3:
                            for col in (0, S_SAMPLE + 1, T + 2):
                                nc.vector.memset(TC[:, col:col + 1], 0.0).then_inc(s_cell, 1)
                        if u == 15:
                            dve.wait_ge(s_cw, 16 * (b["cw"] + 1))
                            dve.wait_ge(s_gated, b["gated"] + 2)
                            nc.vector.tensor_scalar(TA[:, 0:T + 1], TC[:, 1:T + 2], CW[:, 1:2],
                                                    None, ALU.mult).then_inc(s_cell, 1)
                        if u in (17, 19):
                            tap = {17: 0, 19: 2}[u]
                            dve.wait_ge(s_cell, b["cell"] + (14 if tap == 0 else 15))
                            nc.vector.scalar_tensor_tensor(TA[:, 0:T + 1], TC[:, tap:tap + T + 1],
                                                           CW[:, tap:tap + 1], TA[:, 0:T + 1],
                                                           ALU.mult, ALU.add).then_inc(s_cell, 1)

                    attention(b, DIL_UNITS, DIL_OUT, dil_table, convolution)
                at.step("dil", 3)
                with dve.Fori(0, 2) as j:
                    b = at.body("na", j)
                    for block, (Z, factor) in enumerate(((TA, SCALE), (TB, None), (TA, None))):
                        if block == 1:
                            dve.wait_ge(s_cout, 16 * b["cout"])
                        for c, (t0, n) in enumerate(CHUNKS):
                            scale_out(b, 3 * block + c, Z[:, t0:t0 + n], t0, n, c, factor) \
                                .then_inc(s_drained, 1)
                        if block == 0:
                            split_q(b)
                        if block == 1:
                            split_k(b)
                    dve.wait_ge(s_bias_in, 16 * (b["bias_in"] + 4))
                    e3 = EB[:, :, :, :].rearrange("p h r k -> p (h r) k")
                    nc.vector.tensor_tensor(e3, e3, cmask.unsqueeze(1).to_broadcast([P, 28, GRID_W]),
                                            ALU.add).then_inc(s_cell, 1)
                    dve.wait_ge(s_cell, b["cell"] + 1)
                    nc.vector.tensor_copy(IB[:, :, :, :], EB[:, :, 2:12, :]).then_inc(s_cell, 1)
                    dve.wait_ge(s_cell, b["cell"] + 2)
                    nc.vector.memset(IB[0:64, :, 8:10, :], MASKED).then_inc(s_cell, 1)
                    nc.vector.memset(IB[64:128, :, 0:1, :], MASKED).then_inc(s_cell, 1)
                    nc.vector.memset(IB[64:128, :, 9:10, :], MASKED).then_inc(s_cell, 1)
                    dve.wait_ge(s_cell, b["cell"] + 5)
                    split_v(b)
                    attention(b, NA_UNITS, NA_OUT, na_table)
                at.step("na", 2)
                for c, (t0, n) in enumerate(CHUNKS):
                    for i in range(KT):
                        dve.wait_ge(s_mhi, at["mhi"] + (8 * c + i + 1))
                        nc.vector.tensor_tensor(ML[:, i, 0:n], MS[:, i, 0:n],
                                                MH[:, i, 0:n].bitcast(F32), ALU.subtract) \
                            .then_inc(s_mlo, 1)
                    for nb in range(KT):
                        dve.wait_ge(s_group, at["group"] + (8 * c + nb + 1))
                        if c == 2 and nb == 0:
                            dve.wait_ge(s_xl, at["xl"] + 8)
                        nc.vector.tensor_copy(YO[c % 2][:, nb, 0:n], PS[:, nb % 4, 0:n]) \
                            .then_inc(s_drained, 1)
                        if nb == 0:
                            if c == 2:
                                one_over(at, EVENT["x", 0], RS[:, 0:512])
                            if c:
                                one_over(at, EVENT["y", c - 1], RT[:, 0:CHUNKS[c - 1][1]])
                        for k in STEPS[nb] if c else ():
                            step(at, YO[(c - 1) % 2], 0, c - 1, k, 1)
                one_over(at, EVENT["x", 1], RS[:, 512:1024])
                one_over(at, EVENT["y", 2], RT[:, 0:CHUNKS[2][1]])
                for k in ALL_STEPS:
                    step(at, YO[0], 0, 2, k, 1)
                dve.wait_ge(s_xl, at["xl"] + 24)
                dve.wait_ge(s_sq, at["sq"] + 48)
                dve.wait_ge(s_rstd, at["rstd"] + 5)
                end_of_out = EVENT["x", 2]
                out_at = at.after("layer0", 0)
                at.step("out")

                def gate_out(at, g, i, c, bank, up_before):
                    t0, n = CHUNKS[c]
                    scale_out(at, g, SG[:, t0:t0 + n], t0, n, bank) \
                        .then_inc(s_gate, 1)
                    dve.wait_ge(s_gate, at["gate"] + (i + 1))
                    dve.sem_inc(s_drained, 1)

                def hidden_out(at, g, i, t, c, bank, sgr):
                    t0, n = CHUNKS[c]
                    dve.wait_ge(s_group, at["group"] + (g + 1))
                    dve.wait_ge(s_sgr, at["sgr"] + sgr)
                    if i >= 2:
                        dve.wait_ge(s_hl, at["hl"] + (i - 1))
                    nc.vector.tensor_tensor(HT[:, i % 2, 0:n], PS[:, bank, 0:n], SG[:, t0:t0 + n],
                                            ALU.mult).then_inc(s_h, 1)
                    dve.wait_ge(s_h, at["h"] + (i + 1))
                    dve.sem_inc(s_drained, 1)
                    dve.wait_ge(s_hh, at["hh"] + (i + 1))
                    nc.vector.tensor_tensor(HL[t][:, t0:t0 + n], HT[:, i % 2, 0:n],
                                            HH[t][:, t0:t0 + n].bitcast(F32), ALU.subtract) \
                        .then_inc(s_hl, 1)

                def down_out(at, g0, cleared, chunks=(0, 1, 2), turn=0):
                    for c in chunks:
                        t0, n = CHUNKS[c]
                        for nb in range(KT):
                            g = 8 * c + nb
                            dve.wait_ge(s_group, at["group"] + (g0 + g + 1))
                            if g == 0:
                                dve.wait_ge(s_cleared, cleared)
                            nc.vector.tensor_tensor(ACC[:, nb, t0:t0 + n], ACC[:, nb, t0:t0 + n],
                                                    PS[:, 5 + (g + turn) % 3, 0:n], ALU.add) \
                                .then_inc(s_drained, 1)

                for c in range(NCH):
                    if c == 2:
                        one_over(out_at, end_of_out, RS[:, 1024:T])
                        dve.wait_ge(s_rstd, at["rstd"])
                    gate_out(at, c, c, c, c, None)
                at.step("ffn0")
                with dve.Fori(0, 10) as j:
                    b = at.body("ffn", j)
                    for c in range(NCH):
                        hidden_out(b, c, c, 0, c, 3 + c, c - 2)
                    for c in range(NCH):
                        gate_out(b, 3 + c, c, c, c, None)
                    for c in range(NCH):
                        hidden_out(b, 6 + c, 3 + c, 1, c, 3 + c, c + 1)
                    for c in range(NCH):
                        gate_out(b, 9 + c, 3 + c, c, c, None)
                    down_out(b, 12, at["cleared"] + 1)
                at.step("ffn", 10)
                for c in range(NCH):
                    hidden_out(at, c, c, 0, c, 3 + c, c - 2)
                for c in range(NCH):
                    gate_out(at, 3 + c, c, c, c, None)
                for c in range(NCH):
                    hidden_out(at, 6 + c, 3 + c, 1, c, 3 + c, c + 1)
                upd = at.after("ffn1")
                for c in range(NCH):
                    t0, n = CHUNKS[c]
                    down_out(at, 9, at["cleared"] + 1, ((0, 1), (2,), ())[c], 1)
                    if c:
                        pt, pn = CHUNKS[c - 1]
                        one_over(upd, EVENT["x", c - 1], RS[:, pt:pt + pn])
                    one_over(upd, EVENT["y", c], RT[:, 0:n])
                    for k in ALL_STEPS:
                        step(upd, ACC, t0, c, k, 3)
                one_over(upd, EVENT["x", 2], RS[:, 1024:T])
                dve.wait_ge(s_xl, upd["xl"] + 24)
                at.step("ffn1")
                at.step("upd")

        @block.tensor
        def _(pe):
            def products(out, wh, wl, xh, xl, first, last):
                nc.tensor.matmul(out, wh, xh, start=first, stop=False)
                nc.tensor.matmul(out, wh, xl, start=False, stop=False)
                return nc.tensor.matmul(out, wl, xh, start=False, stop=last)

            def group(at, slot_w, g, bank, c, back=3):
                t0, n = CHUNKS[c]
                pe.wait_ge(s_drained, at["drained"] + (g - back + 1))
                for t in range(KT):
                    last = products(PS[:, bank, 0:n], WH[slot_w][:, t, :],
                                    WL[slot_w][:, t, :], XH[:, t, t0:t0 + n],
                                    XL[:, t, t0:t0 + n], t == 0, t == KT - 1)
                last.then_inc(s_group, 1)

            def project(at, k, slot_w, g, banks, x_from=None):
                pe.wait_ge(s_lo, at["lo"] + (k + 1))
                for c in range(NCH):
                    if x_from is not None:
                        pe.wait_ge(s_xl, x_from + 8 * (c + 1))
                    group(at, slot_w, g + c, banks[c], c)

            def sum_partitions(at, order, event, kind, c):
                n = CHUNKS[c][1]
                pe.wait_ge(s_sq, at["sq"] + 1)
                pe.wait_ge(s_part, at["part"] + order.last_add(kind, c))
                if event[kind, c] or at is not START:
                    pe.wait_ge(s_rooted, at["rooted"] + event[kind, c])
                nc.tensor.matmul(PS[:, SUM_BANK, 0:n], ones, SSUM[kind][:, 0:n], start=True,
                                 stop=True).then_inc(s_sumd, 1)

            pe.sem_inc(s_group, 9)
            pe.wait_ge(s_consts, 16)
            pe.wait_ge(s_xin, 16 * TILES)
            for c, (t0, n) in enumerate(CHUNKS):
                for i in range(KT):
                    if 8 * c + i >= 4:
                        pe.wait_ge(s_xl, 8 * c + i - 3)
                    for j in range(n // P):
                        last = nc.tensor.transpose(PS[:, i % 4, j * P:(j + 1) * P],
                                                   XIN[:, t0 // P + j, i * P:(i + 1) * P], ident)
                    last.then_inc(s_turned, 1)
                sum_partitions(START, SQ_IN, EVENT_IN, "x", c)

            def turn_v(b):
                for g, (bank, a, n) in enumerate(VBANKS):
                    for j in range(n):
                        t = a + j
                        last = nc.tensor.transpose(PS[:, bank, j * P:(j + 1) * P],
                                                   TA[:, t * P:(t + 1) * P], ident)
                    last.then_inc(s_vt, 1)

            def attention(b, units, banks, beside=None):
                starts = quad_starts(units)

                def scores(u):
                    i, h, k0, nkt = units[u]
                    if u >= 2:
                        pe.wait_ge(s_masked, b["masked"] + (u - 1))
                    q = QS[h][:, i * P:(i + 1) * P]
                    for a, n in quads(nkt):
                        keys = slice((k0 + a) * P, (k0 + a + n) * P)
                        bank = PS[:, 2 * (u % 2) + a // 4, 0:n * P]
                        nc.tensor.matmul(bank, q, KH[h][:, keys], start=True, stop=False)
                        last = nc.tensor.matmul(bank, q, KL[h][:, keys], start=False, stop=True)
                    last.then_inc(s_scored, 1)

                def turn(u):
                    i, h, k0, nkt = units[u]
                    pe.wait_ge(s_exped, b["exped"] + (u + 1))
                    if u:
                        pe.wait_ge(s_ptl, b["ptl"] + starts[u])
                    for g, (a, n) in enumerate(quads(nkt)):
                        for j in range(n):
                            last = nc.tensor.transpose(
                                PS[:, 4 + g, j * P:(j + 1) * P],
                                PR[:, u % 2, (a + j) * P:(a + j + 1) * P], ident)
                        last.then_inc(s_tp, 1)

                def values(u):
                    i, h, k0, nkt = units[u]
                    back = 2 if banks[0] != banks[1] else 1
                    if u >= back:
                        pe.wait_ge(s_y, b["y"] + (u + 1 - back))
                    if u >= 2 and (back == 1 or u % 2):
                        pe.wait_ge(s_yb, b["yb"] + u // 2)
                    o = PS[:, banks[u % 2], 0:P]
                    for g, (a, n) in enumerate(quads(nkt)):
                        pe.wait_ge(s_ptl, b["ptl"] + (starts[u] + g + 1))
                        for j in range(n):
                            v = V[:, k0 + a + j, h, :]
                            nc.tensor.matmul(o, PTH[u % 2][:, g, j, :], v, start=a + j == 0, stop=False)
                            last = nc.tensor.matmul(o, PTL[u % 2][:, g, j, :], v, start=False,
                                                    stop=a + j == nkt - 1)
                    last.then_inc(s_pv, 1)

                def turn_y(i):
                    pe.wait_ge(s_y, b["y"] + (2 * i + 2))
                    nc.tensor.transpose(PS[:, banks[1], 0:P], YN[:, i % 2, :], ident).then_inc(s_yt, 1)

                pe.wait_ge(s_stack_lo, b["stack_lo"] + 6)
                pe.wait_ge(s_drained, b["drained"] + 9)
                scores(0)
                scores(1)
                turn_v(b)
                pe.wait_ge(s_vl, b["vl"] + 3)
                for u in range(NU):
                    turn(u)
                    if u + 2 < NU:
                        scores(u + 2)
                    if beside is not None:
                        beside(u, 0)
                    if u >= 3 and u % 2:
                        turn_y(u // 2 - 1)
                    if beside is not None:
                        beside(u, 1)
                    if u:
                        values(u - 1)
                values(NU - 1)
                turn_y(TILES - 1)

            with pe.Fori(0, DEPTH) as L:
                at = At(L)
                at.step("layer0")
                with pe.Fori(0, 3) as j:
                    b = at.body("dil", j)
                    for k in range(3):
                        project(b, k, k, 3 * k, (0, 1, 2), at["xl"] - 24 if k == 0 else None)

                    def convolution(u, part):
                        if u >= 18:
                            return
                        g = u // 2
                        k, c = divmod(g, 3)
                        t0, n = CHUNKS[c]
                        if u % 2 == 0 and part == 0:
                            if c == 0:
                                pe.wait_ge(s_lo, b["lo"] + (4 + k))
                            pe.wait_ge(s_drained, b["drained"] + (9 + g))
                        for t in range(4 * (u % 2) + 2 * part, 4 * (u % 2) + 2 * part + 2):
                            last = products(PS[:, 7, 0:n], WH[k][:, t, :], WL[k][:, t, :],
                                            XH[:, t, t0:t0 + n], XL[:, t, t0:t0 + n], t == 0,
                                            t == KT - 1)
                        if u % 2 and part == 1:
                            last.then_inc(s_group, 1)

                    attention(b, DIL_UNITS, DIL_OUT, convolution)
                at.step("dil", 3)
                with pe.Fori(0, 2) as j:
                    b = at.body("na", j)
                    for k in range(3):
                        project(b, k, k, 3 * k, (0, 1, 2))
                    attention(b, NA_UNITS, NA_OUT)
                at.step("na", 2)
                for c, (t0, n) in enumerate(CHUNKS):
                    for nb in range(KT):
                        u = 8 * c + nb
                        pe.wait_ge(s_lo, at["lo"] + (u + 1))
                        pe.wait_ge(s_drained, at["drained"] + (u - 3 + 1))
                        for t in range(KT):
                            if nb == 0:
                                pe.wait_ge(s_mlo, at["mlo"] + (8 * c + t + 1))
                            last = products(PS[:, nb % 4, 0:n], WH[u % 3][:, t, :],
                                            WL[u % 3][:, t, :], MH[:, t, 0:n], ML[:, t, 0:n],
                                            t == 0, t == KT - 1)
                        last.then_inc(s_group, 1)
                        if c and nb == 0:
                            sum_partitions(at, SQ_OUT, EVENT, "y", c - 1)
                    if c:
                        sum_partitions(at, SQ_OUT, EVENT, "x", c - 1)
                ffn = at.after("out")
                pe.wait_ge(s_lo, ffn["lo"] + 1)
                group(ffn, 0, 0, 0, 0)
                sum_partitions(at, SQ_OUT, EVENT, "y", 2)
                group(ffn, 0, 1, 1, 1)
                pe.wait_ge(s_xl, ffn["xl"])
                group(ffn, 0, 2, 2, 2)
                sum_partitions(at, SQ_OUT, EVENT, "x", 2)
                at.step("out")
                at.step("ffn0")

                def down(at, k, g0, hl, chunks=(0, 1, 2), turn=0):
                    pe.wait_ge(s_lo, at["lo"] + (k + 2))
                    for c in chunks:
                        t0, n = CHUNKS[c]
                        pe.wait_ge(s_hl, at["hl"] + (hl + c + 1))
                        for nb in range(KT):
                            g = 8 * c + nb
                            pe.wait_ge(s_drained, at["drained"] + (g0 + g - 3 + 1))
                            for t in range(2):
                                last = products(PS[:, 5 + (g + turn) % 3, 0:n], WH[2 + t][:, nb, :],
                                                WL[2 + t][:, nb, :], HH[t][:, t0:t0 + n],
                                                HL[t][:, t0:t0 + n], t == 0, t == 1)
                            last.then_inc(s_group, 1)

                with pe.Fori(0, 10) as j:
                    b = at.body("ffn", j)
                    project(b, 0, 1, 0, (3, 4, 5))
                    project(b, 1, 0, 3, (0, 1, 2))
                    project(b, 2, 1, 6, (3, 4, 5))
                    project(b, 3, 0, 9, (0, 1, 2))
                    down(b, 4, 12, 3)
                at.step("ffn", 10)
                project(at, 0, 1, 0, (3, 4, 5))
                project(at, 1, 0, 3, (0, 1, 2))
                project(at, 2, 1, 6, (3, 4, 5))
                upd = at.after("ffn1")
                down(at, 3, 9, 3, (0, 1), 1)
                sum_partitions(upd, SQ_UPD, EVENT, "y", 0)
                down(at, 3, 9, 3, (2,), 1)
                sum_partitions(upd, SQ_UPD, EVENT, "x", 0)
                for c in (1, 2):
                    sum_partitions(upd, SQ_UPD, EVENT, "y", c)
                    sum_partitions(upd, SQ_UPD, EVENT, "x", c)
                at.step("ffn1")
                at.step("upd")
            end = At(DEPTH)
            pe.wait_ge(s_xl, end["xl"])
            for i in range(TILES):
                for half in range(2):
                    k = 2 * i + half
                    if k >= 4:
                        pe.wait_ge(s_zo, k - 3)
                    for j in range(4):
                        last = nc.tensor.transpose(PS[:, k % 4, j * P:(j + 1) * P],
                                                   ACC[:, 4 * half + j, i * P:(i + 1) * P], ident)
                    last.then_inc(s_zt, 1)


VBANKS = ((4, 0, 4), (5, 4, 4), (7, 8, 2))
DIL_OUT, NA_OUT = (6, 6), (6, 7)
SUM_BANK = 4
CONV_PARTS = ((0, S_SAMPLE, 1), (S_SAMPLE, S_PROMPT, S_SAMPLE + 2))


def quad_starts(units):
    starts = [0]
    for u in units:
        starts.append(starts[-1] + len(quads(u[3])))
    return starts


def kernel(x_prompt, x_sample, g_pre_mix, w_in, conv_w, rpb, w_out, g_post_mix,
           g_pre_ffn, w_gate, w_up, w_down, g_post_ffn):
    import concourse.bacc as bacc
    from concourse.bass_utils import run_bass_kernel_spmd

    nc = bacc.Bacc("TRN2", target_bir_lowering=False, num_devices=1, dynamic_dma_scratch_size=SCRATCH)
    x = np.concatenate([np.asarray(x_sample)[0], np.asarray(x_prompt)[0]], 0)
    gains = np.stack([np.asarray(g) for g in (g_pre_mix, g_post_mix, g_pre_ffn, g_post_ffn)], 1)
    gains = gains.reshape(DEPTH, 4, KT, P).transpose(0, 3, 1, 2).reshape(DEPTH, P, 4 * KT)
    taps = np.asarray(conv_w).reshape(DEPTH, 3, D_CONV // P, P).transpose(0, 2, 3, 1)
    padded = np.pad(np.asarray(rpb), ((0, 0), (0, 0), (0, 0), (48, 48)))
    windows = np.lib.stride_tricks.sliding_window_view(padded, GRID_W, axis=-1)[..., ::-1, :]
    windows = windows.transpose(0, 1, 3, 2, 4)
    tables, small = constants()
    arrays = {"x": x, "w_in": w_in, "w_out": w_out, "w_gate": w_gate, "w_up": w_up,
              "w_down": w_down, "gains": gains, "conv_w": taps, "rpb": windows,
              "tables": tables, "small": small}
    arrays = {k: np.ascontiguousarray(v) for k, v in arrays.items()}
    args = [nc.dram_tensor(k, v.shape, F32, kind="ExternalInput").ap() for k, v in arrays.items()]
    mixed = nc.dram_tensor("mixed", [KT, P, T], F32, kind="Internal").ap()
    out = nc.dram_tensor("out", [T, D], F32, kind="ExternalOutput").ap()
    build(nc, *args, mixed, out)
    r = run_bass_kernel_spmd(nc, [arrays], core_ids=[0])
    y = r.results[0]["out"]
    return y[S_SAMPLE:][None], y[:S_SAMPLE][None]
```

```python
from contextlib import ExitStack

import numpy as np

import concourse.bass as bass
from concourse import mybir

F32 = mybir.dt.float32
F32R = mybir.dt.float32r
ALU = mybir.AluOpType
ACT = mybir.ActivationFunctionType

P = 128
DEPTH = 2
D = 1024
KT = D // P
S_SAMPLE, S_PROMPT = 1024, 256
T = S_SAMPLE + S_PROMPT
CHUNKS = ((0, 512), (512, 512), (1024, 256))
NCH = len(CHUNKS)
TILES = T // P
HD = 64
D_DIL, D_NA, D_CONV = 384, 256, 384
D_IN = 3 * D
D_FF = 2816
FT = D_FF // P
GRID_W, NA_ROWS, NA_COLS = 64, 8, 16
EPS = 1e-6
SCRATCH = 256
MASKED = -1e30
SCALE = HD ** -0.5

DIL_UNITS = [(i, h, 0, 8) for i in range(8) for h in range(2)] + \
            [(i, h, 8, 2) for i in (8, 9) for h in range(2)]


def na_keys(i):
    if i >= 8:
        return 8, 2
    if i < 2:
        return 0, 4
    if i >= 6:
        return 4, 4
    return i - 2, 5


NA_UNITS = [(i, h) + na_keys(i) for i in range(TILES) for h in range(2)]


def quads(nkt):
    return [(a, min(4, nkt - a)) for a in range(0, nkt, 4)]


N_DQ = sum(len(quads(u[3])) for u in DIL_UNITS)
N_NQ = sum(len(quads(u[3])) for u in NA_UNITS)
NU = len(DIL_UNITS)
LAST = 4
MIXED_ORDER = (0, 1, 2, 3, 5, 6, 7, LAST)

ATT = dict(scored=NU, masked=NU, exped=NU, pv=NU, o_tmp=NU, recip=NU, y=NU, yt=TILES, yb=TILES,
           yout=1, vt=3, vh=3, vl=3, stack_hi=6, stack_lo=6)
UPDATE = dict(sq=48, part=42, sumd=6, rooted=6, rstd=6, joined=24, z=48, xh=24, xl=24)
PER = {
    "layer0": dict(gains=1, gmix=1, tab=1, trip=1, unit=3, gained=3),
    "dil": dict(trip=2, unit=6, gained=6, group=18, tp=N_DQ, pth=N_DQ, ptl=N_DQ, swap=8, cell=16,
                cw=1, cout=1, gated=2, convolved=2, **ATT),
    "na": dict(trip=1, unit=3, gained=3, group=9, tp=N_NQ, pth=N_NQ, ptl=N_NQ, cell=5, bias_in=4,
               **ATT),
    "out": dict(trip=7, unit=21, group=24, mload=6, mlast=3, mhi=24, mlo=24, **UPDATE),
    "ffn0": dict(cleared=1, unit=1, gained=1, group=3, gate=3, sig=3, sgr=3),
    "ffn": dict(trip=2, unit=6, gained=4, group=36, gate=6, sig=6, sgr=6, h=6, hh=6, hl=6),
    "ffn1": dict(unit=5, gained=3, group=33, gate=3, sig=3, sgr=3, h=6, hh=6, hl=6),
    "upd": dict(trip=2, **UPDATE),
}
COUNT = {"layer0": 1, "dil": 3, "na": 2, "out": 1, "ffn0": 1, "ffn": 10, "ffn1": 1, "upd": 1}
FIRST = dict(group=9, gained=1, drained=6, lo=3, cell=1, yout=1, cout=1, sq=24, part=21, sumd=3, rooted=3,
             rstd=3, xh=24, xl=24)
SAME = {"hi": "unit", "lo": "unit", "drained": "group"}
ORDER = list(PER)

STEPS = ((), (0, 1), (2, 3), (4, 5), (6,), (7,), (8,), ())
EARLY = 2
ALL_STEPS = tuple(range(KT + 1))


def squares_out():
    order = []
    for c in range(NCH):
        for nb in range(KT):
            order.append(("y", c, nb))
            if c:
                order += [("x", c - 1, k) for k in STEPS[nb] if k < KT]
    return order + [("x", NCH - 1, k) for k in range(KT)]


def squares_upd():
    order = [("y", 0, k) for k in range(KT)] + [("y", 1, k) for k in range(EARLY)]
    for k in range(EARLY, KT):
        order += [("y", 1, k), ("x", 0, k - EARLY)]
    order += [("x", 0, k) for k in range(KT - EARLY, KT)]
    return order + [(kind, c, k) for kind, c in (("y", 2), ("x", 1), ("x", 2)) for k in range(KT)]


class Squares:

    def __init__(self, order):
        self.sq = {e: n for n, e in enumerate(order)}
        added = [e for e in order if e[2]]
        self.add = {e: n for n, e in enumerate(added)}

    def last_add(self, kind, c):
        return self.add[kind, c, KT - 1] + 1


SQ_OUT, SQ_UPD = Squares(squares_out()), Squares(squares_upd())
SQ_IN = Squares([("x", c, k) for c in range(NCH) for k in range(KT)])
EVENT = {("y", c): 2 * c for c in range(NCH)} | {("x", c): 2 * c + 1 for c in range(NCH)}
EVENT_IN = {("x", c): c for c in range(NCH)}
START = dict.fromkeys(("sq", "part", "sumd", "rooted", "rstd", "xh", "xl"), 0)


class At:

    def __init__(self, layer):
        self.base = {}
        self.names = {k for p in PER.values() for k in p} | set(SAME)
        for k in self.names:
            per = sum(PER[s].get(SAME.get(k, k), 0) * COUNT[s] for s in ORDER)
            self.base[k] = layer * per + FIRST.get(k, 0)

    def __getitem__(self, k):
        return self.base[k]

    def step(self, section, times=1):
        for k in self.names:
            self.base[k] = self.base[k] + times * PER[section].get(SAME.get(k, k), 0)

    def after(self, section, times=1):
        return self.body(section, times)

    def body(self, section, it):
        new = At.__new__(At)
        new.names = self.names
        new.base = {k: self.base[k] + it * PER[section].get(SAME.get(k, k), 0)
                    if PER[section].get(SAME.get(k, k), 0) else self.base[k] for k in self.names}
        return new


def constants():
    f = np.float32
    inv = (f(1.0) / (f(10000.0) ** (np.arange(0, HD, 2, dtype=f) / f(HD)))).astype(f)
    ang = (np.arange(S_SAMPLE, dtype=f)[None, :] * inv[:, None]).astype(f)
    cos, sin = np.cos(ang).astype(f), np.sin(ang).astype(f)
    cos128 = np.concatenate([cos] * 4, 0)
    sin128 = np.concatenate([-sin, sin, -sin, sin], 0)
    d = np.abs(np.arange(1920)[None, :] - 896 - np.arange(P)[:, None])
    count = (d <= 64).astype(int) + ((d % 4 == 0) & (d <= 256)) + (d % 16 == 0)
    log = np.where(count > 0, np.log(np.maximum(count, 1)), MASKED).astype(f)
    qc = np.arange(GRID_W)
    start = np.clip(qc - NA_COLS // 2, 0, GRID_W - NA_COLS)
    ok = (qc[None, :] >= start[:, None]) & (qc[None, :] < start[:, None] + NA_COLS)
    cmask = np.tile(np.where(ok, 0.0, MASKED).astype(f), (2, 1))
    eye_ones = np.concatenate([np.eye(P, dtype=f), np.ones((P, P), f), cmask], 1)
    return np.ascontiguousarray(np.concatenate([log, cos128, sin128], 1)), eye_ones


def build(nc, x, w_in, w_out, w_gate, w_up, w_down, gains, conv_w, rpb, tables, small, mixed, out):
    with ExitStack() as ctx:
        at = [SCRATCH]

        def place(name, shape, dt=F32, offset=None):
            size = int(np.prod(shape[1:])) * 4
            if offset is None:
                offset, at[0] = at[0], at[0] + (size + 31) // 32 * 32
            return nc.alloc_sbuf_tensor_at(name, shape, dt, offset=offset)

        XH = place("XH", [P, KT, T], F32R)
        XL = place("XL", [P, KT, T], F32R)
        X = place("X", [P, KT, T], offset=at[0] - KT * T * 4)
        RS = place("RS", [P, T])
        RAW = [place(f"RAW{s}", [P, KT, P]) for s in range(3)]
        WH, WL = [], []
        for s in range(4):
            WH.append(place(f"WH{s}", [P, KT, P], F32R))
            WL.append(place(f"WL{s}", [P, KT, P], F32R))
        w3 = at[0] - 8192
        EYE = place("EYE", [P, 2 * P + GRID_W])
        ident, ones, cmask = EYE[:, 0:P], EYE[:, P:2 * P], EYE[:, 2 * P:]
        GP = place("GP", [P, 2 * KT])
        GL = place("GL", [P, 3 * KT])
        EPSC = place("EPSC", [P, 1])
        base = at[0]
        STAT = place("STAT", [P, 16])
        CW = STAT[:, 12:15]
        NM = STAT[:, 0:4]
        SM = STAT[:, 4:8]
        RC = STAT[:, 8:12]
        OT = place("OT", [P, 2, HD])
        YN = place("YN", [P, 2, P])
        QS = [place(f"QS{h}", [P, T], F32R) for h in range(2)]
        KH = [place(f"KH{h}", [P, T], F32R) for h in range(2)]
        KL = [place(f"KL{h}", [P, T], F32R) for h in range(2)]
        TA = place("TA", [P, T + 4])
        TB = place("TB", [P, T + 4])
        TC = place("TC", [P, T + 4])
        V = place("V", [P, TILES, 2, P], F32R)
        PR = place("PR", [P, 2, 1024])
        YB = place("YB", [P, T])
        at[0] += 8192
        tab = at[0]
        TAB = place("TAB", [P, 1920 + 2 * 1024])
        assert at[0] <= 229247, at[0]
        EB = place("EB", [P, 2, 14, GRID_W], offset=tab)
        IB = place("IB", [P, 2, 10, GRID_W], offset=tab + 7168)
        PTH = [place("PTH0", [P, 2, 4, P], F32R, offset=w3),
               place("PTH1", [P, 2, 4, P], F32R, offset=tab - 8192)]
        PTL = [place("PTL0", [P, 2, 4, P], F32R, offset=w3 + 4096),
               place("PTL1", [P, 2, 4, P], F32R, offset=tab - 4096)]
        at[0] = base
        SQ = place("SQ", [P, 2, 512])
        SSY = place("SSY", [P, 512])
        SSX = place("SSX", [P, 512])
        SSUM = {"y": SSY, "x": SSX}
        RT = place("RT", [P, 512])
        past_norms = at[0]
        MS = place("MS", [P, KT, 512])
        MH = place("MH", [P, KT, 512], F32R)
        ML = place("ML", [P, KT, 512], F32R)
        YO = [place(f"YO{c}", [P, KT, 512]) for c in range(2)]
        assert at[0] <= 229247, at[0]
        at[0] = past_norms
        ACC = place("ACC", [P, KT, T])
        past_acc = at[0]
        HH = [place(f"HH{j}", [P, T], F32R) for j in range(2)]
        HL = [place(f"HL{j}", [P, T], F32R) for j in range(2)]
        SG = place("SG", [P, T])
        HT = place("HT", [P, 2, 512])
        assert at[0] <= 229247, at[0]
        ZO = place("ZO", [P, 2, D], offset=past_acc)
        XIN = place("XIN", [P, TILES, D], offset=past_norms)

        PS = ctx.enter_context(nc.psum_tensor("PS", [P, 8, 512], F32))

        def sem(name):
            return ctx.enter_context(nc.semaphore(name))

        s_consts = sem("consts")
        s_xin0 = sem("xin0")
        s_xin1 = sem("xin1")
        s_xin2 = sem("xin2")
        s_turned = sem("turned")
        s_started = sem("started")
        s_gains = sem("gains")
        s_gmix = sem("gmix")
        s_tab = sem("tab")
        s_bias_in = sem("bias_in")
        s_cw = sem("cw")
        s_load0 = sem("load0")
        s_load1 = sem("load1")
        s_load2 = sem("load2")
        s_gained = sem("gained")
        s_hi = sem("hi")
        s_lo = sem("lo")
        s_group = sem("group")
        s_drained = sem("drained")
        s_xh = sem("xh")
        s_xl = sem("xl")
        s_sq = sem("sq")
        s_part = sem("part")
        s_sumd = sem("sumd")
        s_rooted = sem("rooted")
        s_rstd = sem("rstd")
        s_joined = sem("joined")
        s_z = sem("z")
        s_cell = sem("cell")
        s_swap = sem("swap")
        s_stack_hi = sem("stack_hi")
        s_stack_lo = sem("stack_lo")
        s_mask_may = sem("mask_may")
        s_gain_may = sem("gain_may")
        s_load_may = sem("load_may")
        s_vt = sem("vt")
        s_vh = sem("vh")
        s_vl = sem("vl")
        s_scored = sem("scored")
        s_masked = sem("masked")
        s_exped = sem("exped")
        s_tp = sem("tp")
        s_pth = sem("pth")
        s_ptl = sem("ptl")
        s_pv = sem("pv")
        s_o_tmp = sem("o_tmp")
        s_recip = sem("recip")
        s_y = sem("y")
        s_yt = sem("yt")
        s_yb = sem("yb")
        s_yout = sem("yout")
        s_mload = sem("mload")
        s_mlast = sem("mlast")
        s_mhi = sem("mhi")
        s_mlo = sem("mlo")
        s_gate = sem("gate")
        s_sig = sem("sig")
        s_sgr = sem("sgr")
        s_h = sem("h")
        s_hh = sem("hh")
        s_hl = sem("hl")
        s_cleared = sem("cleared")
        s_gated = sem("gated")
        s_convolved = sem("convolved")
        s_cout = sem("cout")
        s_zt = sem("zt")
        s_zo = sem("zo")
        s_zout0 = sem("zout0")
        s_zout1 = sem("zout1")
        xins = (s_xin0, s_xin1, s_xin2)
        loads = (s_load0, s_load1, s_load2)
        zouts = (s_zout0, s_zout1)

        wv = {k: w.rearrange("l (t p) n -> l p t n", p=P)
              for k, w in (("in", w_in), ("out", w_out), ("gate", w_gate), ("up", w_up))}

        block = ctx.enter_context(nc.Block())

        @block.sync
        def _(sp):
            sp.dma_start(EYE[:, :], small).then_inc(s_consts, 16)
            for i in range(TILES):
                sp.dma_start(XIN[:, i, :], x[i * P:(i + 1) * P, :]).then_inc(xins[i * P // 512], 16)

            def load(at, k, matrix, L, col, ring=0, apart=False):
                slot = (ring + k) % 3
                sp.wait_ge(s_lo, at["lo"] + (k - 2))
                if apart:
                    sp.sem_inc(s_load_may, 1)
                src = wv[matrix][bass.ds(L, 1), :, :, bass.ds(col, P)]
                sp.dma_start(RAW[slot][:, :, :], src.rearrange("l p t n -> (l p) t n")) \
                    .then_inc(loads[slot], 16)

            def load_down(at, k, L, row):
                slot = (1 + k) % 3
                sp.wait_ge(s_lo, at["lo"] + (k - 2))
                sp.dma_start(RAW[slot][:, :, :].rearrange("p t n -> p (t n)"),
                             w_down[bass.ds(L, 1), bass.ds(row, P), :]
                             .rearrange("l p n -> (l p) n")).then_inc(loads[slot], 16)

            with sp.Fori(0, DEPTH) as L:
                at = At(L)
                sp.wait_ge(s_gained, at["gained"])
                sp.dma_start(GP[:, 0:KT], gains[bass.ds(L, 1), :, 0:KT]
                             .rearrange("l p n -> (l p) n")).then_inc(s_gmix, 16)
                for k, part in enumerate((1, 0, 2)):
                    load(at, k, "in", L, part * D_DIL, apart=True)
                sp.wait_ge(s_xl, at["xl"])
                sp.dma_start(GL[:, :], gains[bass.ds(L, 1), :, KT:].rearrange("l p n -> (l p) n")) \
                    .then_inc(s_gains, 16)
                sp.dma_start(TAB[:, :], tables).then_inc(s_tab, 16)
                at.step("layer0")

                def dil_loads(b, j, following):
                    for k, part in enumerate((1, 2, 0)):
                        load(b, k, "in", L, j * P + (3 * D_DIL + 3 * D_NA + part * D_CONV))
                    sp.wait_ge(s_cell, b["cell"])
                    sp.sem_inc(s_load_may, 1)
                    sp.dma_start(CW, conv_w[bass.ds(L, 1), bass.ds(j, 1), :, :]
                                 .rearrange("l c p w -> (l c p) w")).then_inc(s_cw, 16)
                    for k, col in enumerate(following):
                        load(b, 3 + k, "in", L, col)

                with sp.Fori(0, 2) as j:
                    dil_loads(at.body("dil", j), j, [j * P + (P + part * D_DIL)
                                                     for part in (1, 0, 2)])
                dil_loads(at.body("dil", 2), 2, [3 * D_DIL + part * D_NA for part in (1, 0, 2)])
                at.step("dil", 3)

                def na_loads(b, j, matrix, following):
                    sp.wait_ge(s_masked, b["masked"])
                    sp.sem_inc(s_load_may, 1)
                    for half in range(2):
                        rows = slice(1, 15) if half == 0 else slice(0, 14)
                        for h in range(2):
                            sp.dma_start(
                                EB[64 * half:64 * half + 64, h, :, :],
                                rpb[bass.ds(L, 1), bass.ds(j * 2 + h, 1), :, rows, :]
                                .rearrange("l h q r k -> (l h q) r k")).then_inc(s_bias_in, 16)
                    for k, col in enumerate(following):
                        load(b, k, matrix, L, col)

                na_loads(at.body("na", 0), 0, "in", [P + 3 * D_DIL + part * D_NA
                                                     for part in (1, 0, 2)])
                na_loads(at.body("na", 1), 1, "out", [k * P for k in range(3)])
                at.step("na", 2)
                for c, (t0, n) in enumerate(CHUNKS):
                    if c == 0:
                        sp.wait_ge(s_scored, at["scored"])
                        sp.wait_ge(s_yout, 16 * (at["yout"] - 1))
                        sp.wait_ge(s_cout, 16 * at["cout"])
                    else:
                        sp.wait_ge(s_mlo, at["mlo"] + 8 * c)
                    for b0, b1, done in ((0, LAST, s_mload), (LAST + 1, KT, s_mload),
                                         (LAST, LAST + 1, s_mlast)):
                        if done is s_mlast:
                            sp.wait_ge(s_yout, 16 * at["yout"])
                        sp.dma_start(MS[:, b0:b1, 0:n],
                                     mixed[b0:b1, :, t0:t0 + n].rearrange("b p n -> p b n")) \
                            .then_inc(done, 16)
                    for u in range(8 * c + (3 if c == 0 else 0), 8 * c + 8):
                        load(at, u - 3, "out", L, u % KT * P)
                at.step("out")
                load(at, 0, "gate", L, 0)
                at.step("ffn0")
                with sp.Fori(0, 10) as j:
                    b = at.body("ffn", j)
                    for k, (m, f) in enumerate((("up", 0), ("gate", 1), ("up", 1), ("gate", 2))):
                        load(b, k, m, L, j * (2 * P) + f * P, ring=1)
                    for k in range(2):
                        load_down(b, 4 + k, L, j * (2 * P) + k * P)
                at.step("ffn", 10)
                for k, (m, f) in enumerate((("up", 20), ("gate", 21), ("up", 21))):
                    load(at, k, m, L, f * P, ring=1)
                for k in range(2):
                    load_down(at, 3 + k, L, (20 + k) * P)
                at.step("ffn1")
                at.step("upd")
            for i in range(TILES):
                sp.wait_ge(s_zo, 2 * i + 2)
                sp.dma_start(out[i * P:(i + 1) * P, :], ZO[:, i % 2, :]).then_inc(zouts[i % 2], 16)
            for half in range(2):
                sp.wait_ge(zouts[half], 16 * (TILES // 2))

        @block.gpsimd
        def _(pool):
            def gain(at, k, g, which, ring=0, scale=None):
                slot = (ring + k) % 3
                pool.wait_ge(loads[slot], 16 * (at["trip"] + ((ring + k) // 3 + 1)))
                gcol = GL[:, which * KT - KT:which * KT] if which else GP[:, 0:KT]
                gcol = gcol if scale is None else scale
                if scale is not None:
                    pool.sem_inc(s_gain_may, 1)
                gcol = gcol.unsqueeze(2).to_broadcast([P, KT, P])
                nc.gpsimd.tensor_tensor(RAW[slot][:, :, :], RAW[slot][:, :, :], gcol, ALU.mult) \
                    .then_inc(s_gained, 1)

            def low(at, k, slot_w, ring=0):
                slot = (ring + k) % 3
                pool.wait_ge(s_hi, at["hi"] + (k + 1))
                nc.gpsimd.tensor_tensor(WL[slot_w][:, :, :], RAW[slot][:, :, :],
                                        WH[slot_w][:, :, :].bitcast(F32), ALU.subtract) \
                    .then_inc(s_lo, 1)

            def add_square(at, order, event, kind, c, i):
                if i == 0:
                    return
                n = CHUNKS[c][1]
                k = order.add[kind, c, i]
                pool.wait_ge(s_sq, at["sq"] + (order.sq[kind, c, i] + 1))
                if i > 1:
                    pool.wait_ge(s_part, at["part"] + (order.add[kind, c, i - 1] + 1))
                nc.gpsimd.tensor_tensor(SSUM[kind][:, 0:n], SSUM[kind][:, 0:n], SQ[:, k % 2, 0:n],
                                        ALU.add).then_inc(s_part, 1)

            def join(c, used):
                t0, n = CHUNKS[c]
                for k in range(KT):
                    pool.wait_ge(s_group, used)
                    nc.gpsimd.tensor_tensor(X[:, k, t0:t0 + n],
                                            XL[:, k, t0:t0 + n].bitcast(F32),
                                            XH[:, k, t0:t0 + n].bitcast(F32), ALU.add) \
                        .then_inc(s_joined, 1)

            pool.sem_inc(s_lo, 3)
            pool.sem_inc(s_gained, 1)
            for kind, c, i in SQ_IN.sq:
                add_square(START, SQ_IN, EVENT_IN, kind, c, i)
            with pool.Fori(0, DEPTH) as L:
                at = At(L)
                pool.wait_ge(s_started, 2)
                pool.wait_ge(s_gmix, 16 * (at["gmix"] + 1))
                for k in range(3):
                    gain(at, k, k, 0)
                    low(at, k, k)
                at.step("layer0")
                with pool.Fori(0, 3) as j:
                    b = at.body("dil", j)
                    pool.wait_ge(s_gains, 16 * b["gains"])
                    for k in range(3):
                        gain(b, k, k, 0)
                        low(b, k, k)
                    for k in range(3, 6):
                        gain(b, k, k, 0)
                    low(b, 3, 0)
                    for k, (t0, n, o) in enumerate(CONV_PARTS):
                        pool.wait_ge(s_drained, b["drained"] + 15)
                        pool.wait_ge(s_cell, b["cell"] + 13)
                        nc.gpsimd.tensor_tensor(TC[:, o:o + n], TA[:, t0:t0 + n], TB[:, t0:t0 + n],
                                                ALU.mult).then_inc(s_gated, 1)
                    low(b, 4, 1)
                    low(b, 5, 2)
                    for t0, n, o in CONV_PARTS:
                        pool.wait_ge(s_drained, b["drained"] + 18)
                        pool.wait_ge(s_cell, b["cell"] + 16)
                        nc.gpsimd.tensor_tensor(TB[:, t0:t0 + n], TB[:, t0:t0 + n],
                                                TA[:, o - 1:o - 1 + n], ALU.mult) \
                            .then_inc(s_convolved, 1)
                at.step("dil", 3)
                with pool.Fori(0, 2) as j:
                    b = at.body("na", j)
                    for k in range(3):
                        gain(b, k, k, 0, scale=GP[:, bass.ds(j * KT, KT)])
                        low(b, k, k)
                at.step("na", 2)
                ffn = at.after("out")
                for c in range(NCH):
                    join(c, at["group"])

                def unit_low(u):
                    if 3 <= u < 24:
                        low(at, u - 3, u % 3)
                    if u == 24:
                        gain(ffn, 0, 0, 2)
                        low(ffn, 0, 0)

                for c in range(NCH):
                    for nb in range(KT):
                        add_square(at, SQ_OUT, EVENT, "y", c, nb)
                        unit_low(8 * c + nb + 3)
                        for k in STEPS[nb] if c else ():
                            if k < KT:
                                add_square(at, SQ_OUT, EVENT, "x", c - 1, k)
                for k in range(KT):
                    add_square(at, SQ_OUT, EVENT, "x", NCH - 1, k)
                at.step("out")

                def scaled_gate(at, i, c):
                    t0, n = CHUNKS[c]
                    pool.wait_ge(s_sig, at["sig"] + (i + 1))
                    nc.gpsimd.tensor_tensor(SG[:, t0:t0 + n], SG[:, t0:t0 + n], RS[:, t0:t0 + n],
                                            ALU.mult).then_inc(s_sgr, 1)

                for c in range(NCH):
                    scaled_gate(at, c, c)
                at.step("ffn0")
                with pool.Fori(0, 10) as j:
                    b = at.body("ffn", j)
                    for k, w in ((0, 1), (1, 0), (2, 1)):
                        gain(b, k, k, 2, ring=1)
                        low(b, k, w, ring=1)
                    for c in range(NCH):
                        scaled_gate(b, c, c)
                    gain(b, 3, 3, 2, ring=1)
                    low(b, 3, 0, ring=1)
                    low(b, 4, 2, ring=1)
                    low(b, 5, 3, ring=1)
                    for c in range(NCH):
                        scaled_gate(b, 3 + c, c)
                at.step("ffn", 10)
                for k, w in ((0, 1), (1, 0), (2, 1)):
                    gain(at, k, k, 2, ring=1)
                    low(at, k, w, ring=1)
                for c in range(NCH):
                    scaled_gate(at, c, c)
                low(at, 3, 2, ring=1)
                low(at, 4, 3, ring=1)
                used = at["group"] + 9
                at.step("ffn1")
                for kind, c, i in SQ_UPD.sq:
                    if (kind, c, i) == ("y", 2, 0):
                        pool.wait_ge(s_joined, at["joined"] + KT)
                        join(1, used)
                    if (kind, c, i) == ("x", 1, 0):
                        join(2, used)
                    add_square(at, SQ_UPD, EVENT, kind, c, i)
                at.step("upd")

        @block.scalar
        def _(act):
            def high(at, k, slot_w, free, gained=None, ring=0):
                slot = (ring + k) % 3
                if gained is None:
                    act.wait_ge(loads[slot], 16 * (at["trip"] + ((ring + k) // 3 + 1)))
                else:
                    act.wait_ge(s_gained, at["gained"] + (gained + 1))
                act.wait_ge(s_group, at["group"] + free)
                nc.scalar.activation(WH[slot_w][:, :, :], RAW[slot][:, :, :], ACT.Copy) \
                    .then_inc(s_hi, 1)

            def square(at, order, event, src, kind, c, i):
                n = CHUNKS[c][1]
                if i == 0:
                    if (kind, c - 1) in event:
                        act.wait_ge(s_sumd, at["sumd"] + (event[kind, c - 1] + 1))
                    elif at is not START:
                        act.wait_ge(s_sumd, at["sumd"])
                    dst = SSUM[kind][:, 0:n]
                else:
                    k = order.add[kind, c, i]
                    if k >= 2:
                        act.wait_ge(s_part, at["part"] + (k - 1))
                    elif at is not START:
                        act.wait_ge(s_part, at["part"])
                    dst = SQ[:, k % 2, 0:n]
                nc.scalar.activation(dst, src, ACT.Square).then_inc(s_sq, 1)

            def root(at, event, n):
                act.wait_ge(s_sumd, at["sumd"] + (event + 1))
                if event or at is not START:
                    act.wait_ge(s_rstd, at["rstd"] + event)
                nc.scalar.activation(RT[:, 0:n], PS[:, SUM_BANK, 0:n], ACT.Sqrt, scale=1.0 / D,
                                     bias=EPSC[:, 0:1]).then_inc(s_rooted, 1)

            def new_high(at, order, Y, t_y, c, i):
                t0, n = CHUNKS[c]
                act.wait_ge(s_z, at["z"] + 16 * c + 2 * (i + 1))
                nc.scalar.activation(XH[:, i, t0:t0 + n], Y[:, i, t_y:t_y + n], ACT.Copy) \
                    .then_inc(s_xh, 1)
                square(at, order, EVENT, Y[:, i, t_y:t_y + n], "x", c, i)

            act.wait_ge(s_started, 1)
            for c, (t0, n) in enumerate(CHUNKS):
                for i in range(KT):
                    act.wait_ge(s_turned, 8 * c + i + 1)
                    nc.scalar.activation(XH[:, i, t0:t0 + n], PS[:, XBANKS[i % 4], 0:n], ACT.Copy) \
                        .then_inc(s_xh, 1)
                    square(START, SQ_IN, EVENT_IN, PS[:, XBANKS[i % 4], 0:n], "x", c, i)
                root(START, c, n)

            def split_q(b, src_ready):
                src_ready()
                nc.scalar.activation(QS[0][0:64, :], TA[0:64, 0:T], ACT.Copy).then_inc(s_stack_hi, 1)
                nc.scalar.activation(QS[1][64:128, :], TA[64:128, 0:T], ACT.Copy) \
                    .then_inc(s_stack_hi, 1)

            def split_k(b, src_ready):
                src_ready()
                for h in range(2):
                    own = TB[64 * h:64 * h + 64, 0:T]
                    for half in (h, 1 - h):
                        nc.scalar.activation(KH[h][64 * half:64 * half + 64, :], own, ACT.Copy) \
                            .then_inc(s_stack_hi, 1)

            def swap_halves(b, src, group, cell):
                act.wait_ge(s_drained, b["drained"] + group)
                act.wait_ge(s_cell, b["cell"] + cell)
                for q in range(4):
                    o = q ^ 1
                    nc.scalar.activation(TC[32 * o:32 * o + 32, 0:T], src[32 * q:32 * q + 32, 0:T],
                                         ACT.Copy).then_inc(s_swap, 1)

            def split_v(b, parts):
                for g in parts:
                    bank, a, n = VBANKS[g]
                    act.wait_ge(s_vt, b["vt"] + (g + 1))
                    ps = PS[:, bank, 0:n * P].rearrange("p (t h d) -> p t h d", h=2, d=HD)
                    nc.scalar.activation(V[:, a:a + n, :, 0:HD], ps, ACT.Copy).then_inc(s_vh, 1)

            def attention(b, units, banks, beside):
                starts = quad_starts(units)

                def exp(u):
                    i, h, k0, nkt = units[u]
                    act.wait_ge(s_masked, b["masked"] + (u + 1))
                    nc.scalar.activation(PR[:, u % 2, 0:nkt * P], PR[:, u % 2, 0:nkt * P], ACT.Exp,
                                         scale=-1.0, bias=NM[:, u % 4:u % 4 + 1],
                                         accum_out=SM[:, u % 4:u % 4 + 1]).then_inc(s_exped, 1)

                def o_low(u):
                    act.wait_ge(s_pv, b["pv"] + (u + 1))
                    act.wait_ge(s_recip, b["recip"] + (u + 1))
                    if u >= 2:
                        act.wait_ge(s_y, b["y"] + (u - 1))
                    nc.scalar.activation(OT[:, u % 2, :], PS[:, banks[u % 2], HD:P],
                                         ACT.Copy, scale=RC[:, u % 4:u % 4 + 1]) \
                        .then_inc(s_o_tmp, 1)

                def y_block(i):
                    act.wait_ge(s_yt, b["yt"] + (i + 1))
                    if i == 0:
                        act.wait_ge(s_yout, 16 * b["yout"])
                    nc.scalar.activation(YB[:, i * P:(i + 1) * P],
                                         PS[:, banks[1], 0:P], ACT.Copy) \
                        .then_inc(s_yb, 1)

                split_v(b, (0, 1))
                exp(0)
                split_v(b, (2,))
                for u in range(NU + 2):
                    if u < NU:
                        for g, (a, n) in enumerate(quads(units[u][3])):
                            act.wait_ge(s_tp, b["tp"] + (starts[u] + g + 1))
                            if u >= 2:
                                act.wait_ge(s_pv, b["pv"] + (u - 1))
                            nc.scalar.activation(
                                PTH[u % 2][:, g, 0:n, :].rearrange("p t q -> p (t q)"),
                                PS[:, 4 + g, 0:n * P], ACT.Copy).then_inc(s_pth, 1)
                    if u >= 3 and u % 2:
                        y_block(u // 2 - 1)
                    if u + 1 < NU:
                        exp(u + 1)
                    if 1 <= u <= NU:
                        o_low(u - 1)
                    beside(u)

            def store_block(b, block):
                act.wait_ge(s_yb, b["yb"] + TILES)
                act.dma_start(mixed[bass.ds(block, 1), :, :].rearrange("b p n -> (b p) n"),
                              YB[:, :]).then_inc(s_yout, 16)

            with act.Fori(0, DEPTH) as L:
                at = At(L)
                for k in range(3):
                    high(at, k, k, 3 * k - 6, gained=k)
                at.step("layer0")
                with act.Fori(0, 3) as j:
                    b = at.body("dil", j)
                    swap_halves(b, TB, 3, 0)
                    split_k(b, lambda: act.wait_ge(s_cell, b["cell"] + 5))
                    high(b, 0, 0, 3, gained=0)
                    swap_halves(b, TA, 6, 5)
                    split_q(b, lambda: act.wait_ge(s_cell, b["cell"] + 10))

                    def next_high(u):
                        if u < 2:
                            high(b, 1 + u, 1 + u, 6 + 3 * u, gained=1 + u)
                        for k, when in enumerate((8, 14, 19)):
                            if u == when:
                                high(b, 3 + k, k, 12 + 3 * k, gained=3 + k)

                    attention(b, DIL_UNITS, DIL_OUT, next_high)
                    store_block(b, j)
                    act.wait_ge(s_convolved, b["convolved"] + 2)
                    act.dma_start(mixed[bass.ds(j + 5, 1), :, :].rearrange("b p n -> (b p) n"),
                                  TB[:, 0:T]).then_inc(s_cout, 16)
                at.step("dil", 3)
                with act.Fori(0, 2) as j:
                    b = at.body("na", j)
                    split_k(b, lambda: act.wait_ge(s_drained, b["drained"] + 3))
                    split_q(b, lambda: act.wait_ge(s_drained, b["drained"] + 6))

                    def next_high(u):
                        if u in (2, 5, 8):
                            high(b, u // 3, u // 3, 9, gained=u // 3)

                    attention(b, NA_UNITS, NA_OUT, next_high)
                    store_block(b, j + 3)
                at.step("na", 2)
                ffn = at.after("out")

                def unit_high(u):
                    if u < 24:
                        high(at, u - 3, u % 3, u - 2)
                    if u == 24:
                        high(ffn, 0, 0, -2, gained=0)

                def mixed_high(c):
                    t0, n = CHUNKS[c]
                    act.wait_ge(s_mload, 16 * (at["mload"] + 2 * (c + 1)))
                    act.wait_ge(s_group, at["group"] + 8 * c)
                    for i in MIXED_ORDER:
                        if i == LAST:
                            act.wait_ge(s_mlast, 16 * (at["mlast"] + (c + 1)))
                        nc.scalar.activation(MH[:, i, 0:n], MS[:, i, 0:n], ACT.Copy) \
                            .then_inc(s_mhi, 1)

                mixed_high(0)
                for c, (t0, n) in enumerate(CHUNKS):
                    for nb in range(KT):
                        act.wait_ge(s_drained, at["drained"] + (8 * c + nb + 1))
                        square(at, SQ_OUT, EVENT, YO[c % 2][:, nb, 0:n], "y", c, nb)
                        if nb == KT - 1 and c + 1 < NCH:
                            mixed_high(c + 1)
                        unit_high(8 * c + nb + 3)
                        if c and nb == 0:
                            root(at, EVENT["y", c - 1], CHUNKS[c - 1][1])
                        for k in STEPS[nb] if c else ():
                            if k < KT:
                                new_high(at, SQ_OUT, YO[(c - 1) % 2], 0, c - 1, k)
                    if c:
                        root(at, EVENT["x", c - 1], CHUNKS[c - 1][1])
                root(at, EVENT["y", 2], CHUNKS[2][1])
                for k in range(KT):
                    new_high(at, SQ_OUT, YO[0], 0, 2, k)
                root(at, EVENT["x", 2], CHUNKS[2][1])
                at.step("out")

                def silu(at, i, c):
                    t0, n = CHUNKS[c]
                    act.wait_ge(s_gate, at["gate"] + (i + 1))
                    nc.scalar.activation(SG[:, t0:t0 + n], SG[:, t0:t0 + n], ACT.Silu) \
                        .then_inc(s_sig, 1)

                def hidden_high(at, i, t, c):
                    t0, n = CHUNKS[c]
                    act.wait_ge(s_h, at["h"] + (i + 1))
                    nc.scalar.activation(HH[t][:, t0:t0 + n], HT[:, i % 2, 0:n], ACT.Copy) \
                        .then_inc(s_hh, 1)

                for c in range(NCH):
                    silu(at, c, c)
                at.step("ffn0")
                with act.Fori(0, 10) as j:
                    b = at.body("ffn", j)
                    high(b, 0, 1, -27, gained=0, ring=1)
                    high(b, 1, 0, -24, gained=1, ring=1)
                    for c in range(NCH):
                        hidden_high(b, c, 0, c)
                    high(b, 2, 1, 3, gained=2, ring=1)
                    for c in range(NCH):
                        silu(b, c, c)
                    high(b, 3, 0, 6, gained=3, ring=1)
                    high(b, 4, 2, 0, ring=1)
                    high(b, 5, 3, 0, ring=1)
                    for c in range(NCH):
                        hidden_high(b, 3 + c, 1, c)
                    for c in range(NCH):
                        silu(b, 3 + c, c)
                at.step("ffn", 10)
                high(at, 0, 1, -27, gained=0, ring=1)
                high(at, 1, 0, -24, gained=1, ring=1)
                for c in range(NCH):
                    hidden_high(at, c, 0, c)
                high(at, 2, 1, 3, gained=2, ring=1)
                for c in range(NCH):
                    silu(at, c, c)
                high(at, 3, 2, 0, ring=1)
                high(at, 4, 3, 0, ring=1)
                for c in range(NCH):
                    hidden_high(at, 3 + c, 1, c)
                at.step("ffn1")
                for kind, c, i in SQ_UPD.sq:
                    t0, n = CHUNKS[c]
                    if (kind, c, i) in (("y", 1, EARLY), ("y", 2, 0), ("x", 2, 0)):
                        before = {("y", 1): 0, ("y", 2): 1, ("x", 2): 2}[kind, c]
                        root(at, EVENT["y", before], CHUNKS[before][1])
                    if kind == "x":
                        new_high(at, SQ_UPD, ACC, t0, c, i)
                        if i == KT - 1:
                            root(at, EVENT["x", c], n)
                    else:
                        act.wait_ge(s_drained, at["drained"] + (8 * c + i + 1 - 24))
                        square(at, SQ_UPD, EVENT, ACC[:, i, t0:t0 + n], "y", c, i)
                at.step("upd")
            for i in range(TILES):
                act.wait_ge(s_zt, 2 * i + 2)
                if i >= 2:
                    act.wait_ge(zouts[i % 2], 16 * (i // 2))
                nc.scalar.activation(ZO[:, i % 2, 0:512], PS[:, (2 * i) % 4, :], ACT.Copy) \
                    .then_inc(s_zo, 1)
                nc.scalar.activation(ZO[:, i % 2, 512:1024], PS[:, (2 * i + 1) % 4, :], ACT.Copy) \
                    .then_inc(s_zo, 1)

        @block.vector
        def _(dve):
            def scale_out(b, g, dst, t0, n, bank, factor=None):
                dve.wait_ge(s_group, b["group"] + (g + 1))
                if factor is None:
                    ins = nc.vector.tensor_tensor(dst, PS[:, bank, 0:n], RS[:, t0:t0 + n], ALU.mult)
                else:
                    ins = nc.vector.scalar_tensor_tensor(dst, PS[:, bank, 0:n], factor,
                                                         RS[:, t0:t0 + n], ALU.mult, ALU.mult)
                return ins

            def drain_unit(b, k, dst, factor=None):
                for c, (t0, n) in enumerate(CHUNKS):
                    scale_out(b, 3 * k + c, dst[:, t0:t0 + n], t0, n, QKV_BANKS[k][c], factor) \
                        .then_inc(s_drained, 1)

            def rope(b, X, block, factor):
                dve.wait_ge(s_tab, 16 * (b["tab"]))
                dve.wait_ge(s_swap, b["swap"] + 4 * (block + 1))
                dve.wait_ge(s_drained, b["drained"] + 3 * (block + 1))
                for Z, col in ((X, 1920), (TC, 1920 + 1024)):
                    for t0, n in ((0, S_SAMPLE), (S_SAMPLE, S_PROMPT)):
                        nc.vector.scalar_tensor_tensor(Z[:, t0:t0 + n], Z[:, t0:t0 + n], factor,
                                                       TAB[:, col:col + n], ALU.mult, ALU.mult) \
                            .then_inc(s_cell, 1)
                dve.wait_ge(s_cell, b["cell"] + (5 * block + 4))
                nc.vector.tensor_tensor(X[:, 0:T], X[:, 0:T], TC[:, 0:T], ALU.add).then_inc(s_cell, 1)

            def split_q(b):
                dve.wait_ge(s_stack_hi, b["stack_hi"] + 6)
                nc.vector.tensor_tensor(QS[0][64:128, :], TA[0:64, 0:T], QS[0][0:64, :].bitcast(F32),
                                        ALU.subtract).then_inc(s_stack_lo, 1)
                nc.vector.tensor_tensor(QS[1][0:64, :], TA[64:128, 0:T],
                                        QS[1][64:128, :].bitcast(F32), ALU.subtract) \
                    .then_inc(s_stack_lo, 1)

            def split_k(b):
                for h in range(2):
                    own = slice(64 * h, 64 * h + 64)
                    dve.wait_ge(s_stack_hi, b["stack_hi"] + 2 * (h + 1))
                    for half in (h, 1 - h):
                        nc.vector.tensor_tensor(KL[h][64 * half:64 * half + 64, :], TB[own, 0:T],
                                                KH[h][own, :].bitcast(F32), ALU.subtract) \
                            .then_inc(s_stack_lo, 1)

            def split_v(b):
                for g, (bank, a, n) in enumerate(VBANKS):
                    dve.wait_ge(s_vh, b["vh"] + (g + 1))
                    ps = PS[:, bank, 0:n * P].rearrange("p (t h d) -> p t h d", h=2, d=HD)
                    nc.vector.tensor_tensor(V[:, a:a + n, :, HD:P], ps,
                                            V[:, a:a + n, :, 0:HD].bitcast(F32), ALU.subtract) \
                        .then_inc(s_vl, 1)

            def attention(b, units, banks, table, beside=None):
                starts = quad_starts(units)

                def mask(u):
                    i, h, k0, nkt = units[u]
                    dve.wait_ge(s_scored, b["scored"] + (u + 1))
                    if u >= 2:
                        dve.wait_ge(s_tp, b["tp"] + starts[u - 1])
                    dve.sem_inc(s_mask_may, 1)
                    ps = PS[:, 2 * (u % 2):2 * (u % 2) + 2, :].rearrange("p b n -> p (b n)")
                    nc.vector.tensor_tensor_reduce(PR[:, u % 2, 0:nkt * P], ps[:, 0:nkt * P],
                                                   table(i, h, nkt), -1.0, 3e38, ALU.add, ALU.min,
                                                   NM[:, u % 4:u % 4 + 1]).then_inc(s_masked, 1)

                def normalise(u):
                    i, h, k0, nkt = units[u]
                    dve.wait_ge(s_o_tmp, b["o_tmp"] + (u + 1))
                    if h == 0 and i >= 2:
                        dve.wait_ge(s_yt, b["yt"] + (i - 1))
                    nc.vector.scalar_tensor_tensor(YN[:, i % 2, h * HD:h * HD + HD],
                                                   PS[:, banks[u % 2], 0:HD],
                                                   RC[:, u % 4:u % 4 + 1], OT[:, u % 2, :],
                                                   ALU.mult, ALU.add).then_inc(s_y, 1)

                mask(0)
                split_v(b)
                mask(1)
                for u in range(NU + 1):
                    if beside is not None:
                        beside(u)
                    if u < NU:
                        for g, (a, n) in enumerate(quads(units[u][3])):
                            dve.wait_ge(s_pth, b["pth"] + (starts[u] + g + 1))
                            high = PTH[u % 2][:, g, 0:n, :].rearrange("p t q -> p (t q)")
                            nc.vector.tensor_tensor(
                                PTL[u % 2][:, g, 0:n, :].rearrange("p t q -> p (t q)"),
                                PS[:, 4 + g, 0:n * P], high.bitcast(F32), ALU.subtract) \
                                .then_inc(s_ptl, 1)
                    if u + 2 < NU:
                        mask(u + 2)
                    if u < NU:
                        dve.wait_ge(s_exped, b["exped"] + (u + 1))
                        nc.vector.reciprocal(RC[:, u % 4:u % 4 + 1], SM[:, u % 4:u % 4 + 1]) \
                            .then_inc(s_recip, 1)
                    if u >= 1:
                        normalise(u - 1)

            def one_over(at, event, dst):
                dve.wait_ge(s_rooted, at["rooted"] + (event + 1))
                nc.vector.reciprocal(dst, RT[:, 0:dst.shape[1]]).then_inc(s_rstd, 1)

            def step(at, Y, t_y, c, k, which):
                t0, n = CHUNKS[c]
                if k == 0:
                    dve.wait_ge(s_rstd, at["rstd"] + (EVENT["y", c] + 1))
                if k < KT:
                    z = Y[:, k, t_y:t_y + n]
                    nz = at["z"] + (16 * c + 2 * k)
                    nc.vector.scalar_tensor_tensor(z, z, GL[:, which * KT - KT + k:which * KT - KT + k + 1],
                                                   RT[:, 0:n], ALU.mult, ALU.mult).then_inc(s_z, 1)
                    dve.wait_ge(s_joined, at["joined"] + (8 * c + k + 1))
                    dve.wait_ge(s_z, nz + 1)
                    nc.vector.tensor_tensor(z, z, X[:, k, t0:t0 + n], ALU.add) \
                        .then_inc(s_z, 1)
                if k:
                    i = k - 1
                    dve.wait_ge(s_xh, at["xh"] + (8 * c + i + 1))
                    nc.vector.tensor_tensor(XL[:, i, t0:t0 + n], Y[:, i, t_y:t_y + n],
                                            XH[:, i, t0:t0 + n].bitcast(F32), ALU.subtract) \
                        .then_inc(s_xl, 1)

            nc.vector.memset(EPSC[:, :], EPS).then_inc(s_started, 1)
            nc.vector.memset(GP[:, KT:], 1.0).then_inc(s_started, 1)
            dve.sem_inc(s_drained, 6)
            dve.sem_inc(s_cell, 1)
            dve.sem_inc(s_yout, 16)
            dve.sem_inc(s_cout, 16)
            for c, (t0, n) in enumerate(CHUNKS):
                for i in range(KT):
                    dve.wait_ge(s_sq, 8 * c + i + 1)
                    nc.vector.tensor_tensor(XL[:, i, t0:t0 + n], PS[:, XBANKS[i % 4], 0:n],
                                            XH[:, i, t0:t0 + n].bitcast(F32), ALU.subtract) \
                        .then_inc(s_xl, 1)
                one_over(START, c, RS[:, t0:t0 + n])

            def dil_table(i, h, nkt):
                t = i if i < 8 else i - 8
                return TAB[:, 896 - P * t:896 - P * t + nkt * P]

            def na_table(i, h, nkt):
                if 2 <= i < 6:
                    return IB[:, h, :, :].rearrange("p r k -> p (r k)")
                t = i if i < 8 else i - 8
                e = 6 + 2 * (na_keys(i)[0] % 8 - t)
                return EB[:, h, e:e + 2 * nkt, :].rearrange("p r k -> p (r k)")

            with dve.Fori(0, DEPTH) as L:
                at = At(L)
                at.step("layer0")
                with dve.Fori(0, 3) as j:
                    b = at.body("dil", j)
                    dve.wait_ge(s_rstd, b["rstd"])
                    dve.wait_ge(s_cout, 16 * b["cout"])
                    drain_unit(b, 0, TB)
                    rope(b, TB, 0, 1.0)
                    drain_unit(b, 1, TA)
                    split_k(b)
                    rope(b, TA, 1, SCALE)
                    split_q(b)
                    dve.wait_ge(s_stack_lo, b["stack_lo"] + 6)
                    drain_unit(b, 2, TA)

                    def convolution(u):
                        if 2 <= u < 20 and u % 2 == 0:
                            g = u // 2 - 1
                            t0, n = CHUNKS[g % 3]
                            Z = (TA, TB, TB)[g // 3]
                            if g == 6:
                                dve.wait_ge(s_gated, b["gated"] + 2)
                            scale_out(b, 9 + g, Z[:, t0:t0 + n], t0, n, 7).then_inc(s_drained, 1)
                        if u == 3:
                            for col in (0, S_SAMPLE + 1, T + 2):
                                nc.vector.memset(TC[:, col:col + 1], 0.0).then_inc(s_cell, 1)
                        if u == 15:
                            dve.wait_ge(s_cw, 16 * (b["cw"] + 1))
                            dve.wait_ge(s_gated, b["gated"] + 2)
                            nc.vector.tensor_scalar(TA[:, 0:T + 1], TC[:, 1:T + 2], CW[:, 1:2],
                                                    None, ALU.mult).then_inc(s_cell, 1)
                        if u in (17, 19):
                            tap = {17: 0, 19: 2}[u]
                            dve.wait_ge(s_cell, b["cell"] + (14 if tap == 0 else 15))
                            nc.vector.scalar_tensor_tensor(TA[:, 0:T + 1], TC[:, tap:tap + T + 1],
                                                           CW[:, tap:tap + 1], TA[:, 0:T + 1],
                                                           ALU.mult, ALU.add).then_inc(s_cell, 1)

                    attention(b, DIL_UNITS, DIL_OUT, dil_table, convolution)
                at.step("dil", 3)
                with dve.Fori(0, 2) as j:
                    b = at.body("na", j)
                    dve.wait_ge(s_cout, 16 * b["cout"])
                    drain_unit(b, 0, TB)
                    drain_unit(b, 1, TA, SCALE)
                    split_k(b)
                    split_q(b)
                    dve.wait_ge(s_stack_lo, b["stack_lo"] + 6)
                    drain_unit(b, 2, TA)
                    dve.wait_ge(s_bias_in, 16 * (b["bias_in"] + 4))
                    e3 = EB[:, :, :, :].rearrange("p h r k -> p (h r) k")
                    nc.vector.tensor_tensor(e3, e3, cmask.unsqueeze(1).to_broadcast([P, 28, GRID_W]),
                                            ALU.add).then_inc(s_cell, 1)
                    dve.wait_ge(s_cell, b["cell"] + 1)
                    nc.vector.tensor_copy(IB[:, :, :, :], EB[:, :, 2:12, :]).then_inc(s_cell, 1)
                    dve.wait_ge(s_cell, b["cell"] + 2)
                    nc.vector.memset(IB[0:64, :, 8:10, :], MASKED).then_inc(s_cell, 1)
                    nc.vector.memset(IB[64:128, :, 0:1, :], MASKED).then_inc(s_cell, 1)
                    nc.vector.memset(IB[64:128, :, 9:10, :], MASKED).then_inc(s_cell, 1)
                    dve.wait_ge(s_cell, b["cell"] + 5)
                    attention(b, NA_UNITS, NA_OUT, na_table)
                at.step("na", 2)
                for c, (t0, n) in enumerate(CHUNKS):
                    for k, i in enumerate(MIXED_ORDER):
                        dve.wait_ge(s_mhi, at["mhi"] + (8 * c + k + 1))
                        nc.vector.tensor_tensor(ML[:, i, 0:n], MS[:, i, 0:n],
                                                MH[:, i, 0:n].bitcast(F32), ALU.subtract) \
                            .then_inc(s_mlo, 1)
                    for nb in range(KT):
                        dve.wait_ge(s_group, at["group"] + (8 * c + nb + 1))
                        if c == 2 and nb == 0:
                            dve.wait_ge(s_xl, at["xl"] + 8)
                        nc.vector.tensor_copy(YO[c % 2][:, nb, 0:n], PS[:, nb % 4, 0:n]) \
                            .then_inc(s_drained, 1)
                        if nb == 0:
                            if c == 2:
                                one_over(at, EVENT["x", 0], RS[:, 0:512])
                            if c:
                                one_over(at, EVENT["y", c - 1], RT[:, 0:CHUNKS[c - 1][1]])
                        for k in STEPS[nb] if c else ():
                            step(at, YO[(c - 1) % 2], 0, c - 1, k, 1)
                one_over(at, EVENT["x", 1], RS[:, 512:1024])
                one_over(at, EVENT["y", 2], RT[:, 0:CHUNKS[2][1]])
                for k in ALL_STEPS:
                    step(at, YO[0], 0, 2, k, 1)
                dve.wait_ge(s_xl, at["xl"] + 24)
                dve.wait_ge(s_sq, at["sq"] + 48)
                dve.wait_ge(s_rstd, at["rstd"] + 5)
                end_of_out = EVENT["x", 2]
                out_at = at.after("layer0", 0)
                at.step("out")

                def gate_out(at, g, i, c, bank, up_before):
                    t0, n = CHUNKS[c]
                    scale_out(at, g, SG[:, t0:t0 + n], t0, n, bank) \
                        .then_inc(s_gate, 1)
                    dve.wait_ge(s_gate, at["gate"] + (i + 1))
                    dve.sem_inc(s_drained, 1)

                def hidden_out(at, g, i, t, c, bank, sgr):
                    t0, n = CHUNKS[c]
                    dve.wait_ge(s_group, at["group"] + (g + 1))
                    dve.wait_ge(s_sgr, at["sgr"] + sgr)
                    if i >= 2:
                        dve.wait_ge(s_hl, at["hl"] + (i - 1))
                    nc.vector.tensor_tensor(HT[:, i % 2, 0:n], PS[:, bank, 0:n], SG[:, t0:t0 + n],
                                            ALU.mult).then_inc(s_h, 1)
                    dve.wait_ge(s_h, at["h"] + (i + 1))
                    dve.sem_inc(s_drained, 1)
                    dve.wait_ge(s_hh, at["hh"] + (i + 1))
                    nc.vector.tensor_tensor(HL[t][:, t0:t0 + n], HT[:, i % 2, 0:n],
                                            HH[t][:, t0:t0 + n].bitcast(F32), ALU.subtract) \
                        .then_inc(s_hl, 1)

                def down_out(at, g0, cleared, groups=range(3 * KT), turn=0):
                    for g in groups:
                        c, nb = divmod(g, KT)
                        t0, n = CHUNKS[c]
                        dve.wait_ge(s_group, at["group"] + (g0 + g + 1))
                        if g == 0:
                            dve.wait_ge(s_cleared, cleared)
                        nc.vector.tensor_tensor(ACC[:, nb, t0:t0 + n], ACC[:, nb, t0:t0 + n],
                                                PS[:, 5 + (g + turn) % 3, 0:n], ALU.add) \
                            .then_inc(s_drained, 1)

                for c in range(NCH):
                    if c == 2:
                        one_over(out_at, end_of_out, RS[:, 1024:T])
                        dve.wait_ge(s_rstd, at["rstd"])
                    gate_out(at, c, c, c, c, None)
                nc.vector.memset(ACC[:, :, :], 0.0).then_inc(s_cleared, 1)
                at.step("ffn0")
                with dve.Fori(0, 10) as j:
                    b = at.body("ffn", j)
                    for c in range(NCH):
                        hidden_out(b, c, c, 0, c, 3 + c, c - 2)
                    for c in range(NCH):
                        gate_out(b, 3 + c, c, c, c, None)
                    for c in range(NCH):
                        hidden_out(b, 6 + c, 3 + c, 1, c, 3 + c, c + 1)
                    for c in range(NCH):
                        gate_out(b, 9 + c, 3 + c, c, c, None)
                    down_out(b, 12, at["cleared"])
                at.step("ffn", 10)
                for c in range(NCH):
                    hidden_out(at, c, c, 0, c, 3 + c, c - 2)
                for c in range(NCH):
                    gate_out(at, 3 + c, c, c, c, None)
                for c in range(NCH):
                    hidden_out(at, 6 + c, 3 + c, 1, c, 3 + c, c + 1)
                upd = at.after("ffn1")
                for k in range(KT):
                    down_out(at, 9, at["cleared"], (k,), 1)
                    nc.vector.tensor_tensor(X[:, k, 0:512], XL[:, k, 0:512].bitcast(F32),
                                            XH[:, k, 0:512].bitcast(F32), ALU.add) \
                        .then_inc(s_joined, 1)
                down_out(at, 9, at["cleared"], range(KT, KT + EARLY), 1)
                one_over(upd, EVENT["y", 0], RT[:, 0:512])
                for k in range(2 * KT - EARLY):
                    down_out(at, 9, at["cleared"], (KT + EARLY + k,), 1)
                    if k <= KT:
                        step(upd, ACC, 0, 0, k, 3)
                for c in (1, 2):
                    t0, n = CHUNKS[c]
                    pt, pn = CHUNKS[c - 1]
                    one_over(upd, EVENT["x", c - 1], RS[:, pt:pt + pn])
                    one_over(upd, EVENT["y", c], RT[:, 0:n])
                    for k in ALL_STEPS:
                        step(upd, ACC, t0, c, k, 3)
                one_over(upd, EVENT["x", 2], RS[:, 1024:T])
                dve.wait_ge(s_xl, upd["xl"] + 24)
                at.step("ffn1")
                at.step("upd")

        @block.tensor
        def _(pe):
            def products(out, wh, wl, xh, xl, first, last):
                nc.tensor.matmul(out, wh, xh, start=first, stop=False)
                nc.tensor.matmul(out, wh, xl, start=False, stop=False)
                return nc.tensor.matmul(out, wl, xh, start=False, stop=last)

            def group(at, slot_w, g, bank, c, back=3):
                t0, n = CHUNKS[c]
                pe.wait_ge(s_drained, at["drained"] + (g - back + 1))
                for t in range(KT):
                    last = products(PS[:, bank, 0:n], WH[slot_w][:, t, :],
                                    WL[slot_w][:, t, :], XH[:, t, t0:t0 + n],
                                    XL[:, t, t0:t0 + n], t == 0, t == KT - 1)
                last.then_inc(s_group, 1)

            def project(at, k, slot_w, g, banks, x_from=None, back=3):
                pe.wait_ge(s_lo, at["lo"] + (k + 1))
                for c in range(NCH):
                    if x_from is not None:
                        pe.wait_ge(s_xl, x_from + 8 * (c + 1))
                    group(at, slot_w, g + c, banks[c], c, back)

            def sum_partitions(at, order, event, kind, c):
                n = CHUNKS[c][1]
                pe.wait_ge(s_sq, at["sq"] + 1)
                pe.wait_ge(s_part, at["part"] + order.last_add(kind, c))
                if event[kind, c] or at is not START:
                    pe.wait_ge(s_rooted, at["rooted"] + event[kind, c])
                nc.tensor.matmul(PS[:, SUM_BANK, 0:n], ones, SSUM[kind][:, 0:n], start=True,
                                 stop=True).then_inc(s_sumd, 1)

            pe.sem_inc(s_group, 9)
            pe.wait_ge(s_consts, 16)
            for c, (t0, n) in enumerate(CHUNKS):
                pe.wait_ge(xins[c], 16 * (n // P))
                for i in range(KT):
                    if 8 * c + i >= 4:
                        pe.wait_ge(s_xl, 8 * c + i - 3)
                    for j in range(n // P):
                        last = nc.tensor.transpose(PS[:, XBANKS[i % 4], j * P:(j + 1) * P],
                                                   XIN[:, t0 // P + j, i * P:(i + 1) * P], ident)
                    last.then_inc(s_turned, 1)
                sum_partitions(START, SQ_IN, EVENT_IN, "x", c)

            def turn_v(b):
                for g, (bank, a, n) in enumerate(VBANKS):
                    if g == 2:
                        pe.wait_ge(s_vl, b["vl"] + 1)
                    for j in range(n):
                        t = a + j
                        last = nc.tensor.transpose(PS[:, bank, j * P:(j + 1) * P],
                                                   TA[:, t * P:(t + 1) * P], ident)
                    last.then_inc(s_vt, 1)

            def attention(b, units, banks, beside=None):
                starts = quad_starts(units)

                def scores(u):
                    i, h, k0, nkt = units[u]
                    if u >= 2:
                        pe.wait_ge(s_masked, b["masked"] + (u - 1))
                    q = QS[h][:, i * P:(i + 1) * P]
                    for a, n in quads(nkt):
                        keys = slice((k0 + a) * P, (k0 + a + n) * P)
                        bank = PS[:, 2 * (u % 2) + a // 4, 0:n * P]
                        nc.tensor.matmul(bank, q, KH[h][:, keys], start=True, stop=False)
                        last = nc.tensor.matmul(bank, q, KL[h][:, keys], start=False, stop=True)
                    last.then_inc(s_scored, 1)

                def turn(u):
                    i, h, k0, nkt = units[u]
                    pe.wait_ge(s_exped, b["exped"] + (u + 1))
                    if u:
                        pe.wait_ge(s_ptl, b["ptl"] + starts[u])
                    for g, (a, n) in enumerate(quads(nkt)):
                        for j in range(n):
                            last = nc.tensor.transpose(
                                PS[:, 4 + g, j * P:(j + 1) * P],
                                PR[:, u % 2, (a + j) * P:(a + j + 1) * P], ident)
                        last.then_inc(s_tp, 1)

                def values(u):
                    i, h, k0, nkt = units[u]
                    back = 2 if banks[0] != banks[1] else 1
                    if u >= back:
                        pe.wait_ge(s_y, b["y"] + (u + 1 - back))
                    if u >= 2 and (back == 1 or u % 2):
                        pe.wait_ge(s_yb, b["yb"] + u // 2)
                    o = PS[:, banks[u % 2], 0:P]
                    for g, (a, n) in enumerate(quads(nkt)):
                        pe.wait_ge(s_ptl, b["ptl"] + (starts[u] + g + 1))
                        for j in range(n):
                            v = V[:, k0 + a + j, h, :]
                            nc.tensor.matmul(o, PTH[u % 2][:, g, j, :], v, start=a + j == 0, stop=False)
                            last = nc.tensor.matmul(o, PTL[u % 2][:, g, j, :], v, start=False,
                                                    stop=a + j == nkt - 1)
                    last.then_inc(s_pv, 1)

                def turn_y(i):
                    pe.wait_ge(s_y, b["y"] + (2 * i + 2))
                    nc.tensor.transpose(PS[:, banks[1], 0:P], YN[:, i % 2, :], ident).then_inc(s_yt, 1)

                pe.wait_ge(s_stack_lo, b["stack_lo"] + 6)
                pe.wait_ge(s_drained, b["drained"] + 9)
                scores(0)
                scores(1)
                turn_v(b)
                for u in range(NU):
                    turn(u)
                    if u == 0:
                        pe.wait_ge(s_vl, b["vl"] + 3)
                    if u + 2 < NU:
                        scores(u + 2)
                    if beside is not None:
                        beside(u, 0)
                    if u >= 3 and u % 2:
                        turn_y(u // 2 - 1)
                    if beside is not None:
                        beside(u, 1)
                    if u:
                        values(u - 1)
                values(NU - 1)
                turn_y(TILES - 1)

            with pe.Fori(0, DEPTH) as L:
                at = At(L)
                at.step("layer0")
                with pe.Fori(0, 3) as j:
                    b = at.body("dil", j)
                    for k in range(3):
                        project(b, k - 3, k, 3 * k, QKV_BANKS[k], at["xl"] - 24 if k == 0 else None, 6)

                    def convolution(u, part):
                        if u >= 18:
                            return
                        g = u // 2
                        k, c = divmod(g, 3)
                        t0, n = CHUNKS[c]
                        if u % 2 == 0 and part == 0:
                            if c == 0:
                                pe.wait_ge(s_lo, b["lo"] + (1 + k))
                            pe.wait_ge(s_drained, b["drained"] + (9 + g))
                        for t in range(4 * (u % 2) + 2 * part, 4 * (u % 2) + 2 * part + 2):
                            last = products(PS[:, 7, 0:n], WH[k][:, t, :], WL[k][:, t, :],
                                            XH[:, t, t0:t0 + n], XL[:, t, t0:t0 + n], t == 0,
                                            t == KT - 1)
                        if u % 2 and part == 1:
                            last.then_inc(s_group, 1)

                    attention(b, DIL_UNITS, DIL_OUT, convolution)
                at.step("dil", 3)
                with pe.Fori(0, 2) as j:
                    b = at.body("na", j)
                    for k in range(3):
                        project(b, k - 3, k, 3 * k, QKV_BANKS[k], None, 6)
                    attention(b, NA_UNITS, NA_OUT)
                at.step("na", 2)
                for c, (t0, n) in enumerate(CHUNKS):
                    for nb in range(KT):
                        u = 8 * c + nb
                        pe.wait_ge(s_lo, at["lo"] + (u - 3 + 1))
                        pe.wait_ge(s_drained, at["drained"] + (u - 3 + 1))
                        for k, t in enumerate(MIXED_ORDER):
                            if nb == 0:
                                pe.wait_ge(s_mlo, at["mlo"] + (8 * c + k + 1))
                            last = products(PS[:, nb % 4, 0:n], WH[u % 3][:, t, :],
                                            WL[u % 3][:, t, :], MH[:, t, 0:n], ML[:, t, 0:n],
                                            k == 0, k == KT - 1)
                        last.then_inc(s_group, 1)
                        if c and nb == 0:
                            sum_partitions(at, SQ_OUT, EVENT, "y", c - 1)
                    if c:
                        sum_partitions(at, SQ_OUT, EVENT, "x", c - 1)
                ffn = at.after("out")
                pe.wait_ge(s_lo, ffn["lo"] + 1)
                pe.wait_ge(s_xl, ffn["xl"] - 16)
                group(ffn, 0, 0, 0, 0)
                sum_partitions(at, SQ_OUT, EVENT, "y", 2)
                pe.wait_ge(s_xl, ffn["xl"] - 8)
                group(ffn, 0, 1, 1, 1)
                pe.wait_ge(s_xl, ffn["xl"])
                group(ffn, 0, 2, 2, 2)
                sum_partitions(at, SQ_OUT, EVENT, "x", 2)
                at.step("out")
                at.step("ffn0")

                def down(at, k, g0, hl, groups=range(3 * KT), turn=0):
                    for g in groups:
                        c, nb = divmod(g, KT)
                        t0, n = CHUNKS[c]
                        if g == 0:
                            pe.wait_ge(s_lo, at["lo"] + (k + 2))
                        if nb == 0:
                            pe.wait_ge(s_hl, at["hl"] + (hl + c + 1))
                        pe.wait_ge(s_drained, at["drained"] + (g0 + g - 3 + 1))
                        for t in range(2):
                            last = products(PS[:, 5 + (g + turn) % 3, 0:n], WH[2 + t][:, nb, :],
                                            WL[2 + t][:, nb, :], HH[t][:, t0:t0 + n],
                                            HL[t][:, t0:t0 + n], t == 0, t == 1)
                        last.then_inc(s_group, 1)

                with pe.Fori(0, 10) as j:
                    b = at.body("ffn", j)
                    project(b, 0, 1, 0, (3, 4, 5))
                    project(b, 1, 0, 3, (0, 1, 2))
                    project(b, 2, 1, 6, (3, 4, 5))
                    project(b, 3, 0, 9, (0, 1, 2))
                    down(b, 4, 12, 3)
                at.step("ffn", 10)
                project(at, 0, 1, 0, (3, 4, 5))
                project(at, 1, 0, 3, (0, 1, 2))
                project(at, 2, 1, 6, (3, 4, 5))
                upd = at.after("ffn1")
                down(at, 3, 9, 3, range(KT + EARLY), 1)
                sum_partitions(upd, SQ_UPD, EVENT, "y", 0)
                down(at, 3, 9, 3, range(KT + EARLY, 3 * KT), 1)
                sum_partitions(upd, SQ_UPD, EVENT, "x", 0)
                for c in (1, 2):
                    sum_partitions(upd, SQ_UPD, EVENT, "y", c)
                    sum_partitions(upd, SQ_UPD, EVENT, "x", c)
                at.step("ffn1")
                at.step("upd")
            end = At(DEPTH)
            pe.wait_ge(s_xl, end["xl"])
            for i in range(TILES):
                for half in range(2):
                    k = 2 * i + half
                    if k >= 4:
                        pe.wait_ge(s_zo, k - 3)
                    for j in range(4):
                        last = nc.tensor.transpose(PS[:, k % 4, j * P:(j + 1) * P],
                                                   ACC[:, 4 * half + j, i * P:(i + 1) * P], ident)
                    last.then_inc(s_zt, 1)


VBANKS = ((6, 0, 4), (7, 4, 4), (6, 8, 2))
DIL_OUT, NA_OUT = (6, 6), (6, 7)
XBANKS = (3, 5, 6, 7)
QKV_BANKS = ((0, 1, 2), (3, 4, 5), (0, 1, 2))
SUM_BANK = 4
CONV_PARTS = ((0, S_SAMPLE, 1), (S_SAMPLE, S_PROMPT, S_SAMPLE + 2))


def quad_starts(units):
    starts = [0]
    for u in units:
        starts.append(starts[-1] + len(quads(u[3])))
    return starts


def kernel(x_prompt, x_sample, g_pre_mix, w_in, conv_w, rpb, w_out, g_post_mix,
           g_pre_ffn, w_gate, w_up, w_down, g_post_ffn):
    import concourse.bacc as bacc
    from concourse.bass_utils import run_bass_kernel_spmd

    nc = bacc.Bacc("TRN2", target_bir_lowering=False, num_devices=1, dynamic_dma_scratch_size=SCRATCH)
    x = np.concatenate([np.asarray(x_sample)[0], np.asarray(x_prompt)[0]], 0)
    gains = np.stack([np.asarray(g) for g in (g_pre_mix, g_post_mix, g_pre_ffn, g_post_ffn)], 1)
    gains = gains.reshape(DEPTH, 4, KT, P).transpose(0, 3, 1, 2).reshape(DEPTH, P, 4 * KT)
    taps = np.asarray(conv_w).reshape(DEPTH, 3, D_CONV // P, P).transpose(0, 2, 3, 1)
    padded = np.pad(np.asarray(rpb), ((0, 0), (0, 0), (0, 0), (48, 48)))
    windows = np.lib.stride_tricks.sliding_window_view(padded, GRID_W, axis=-1)[..., ::-1, :]
    windows = windows.transpose(0, 1, 3, 2, 4)
    tables, small = constants()
    arrays = {"x": x, "w_in": w_in, "w_out": w_out, "w_gate": w_gate, "w_up": w_up,
              "w_down": w_down, "gains": gains, "conv_w": taps, "rpb": windows,
              "tables": tables, "small": small}
    arrays = {k: np.ascontiguousarray(v) for k, v in arrays.items()}
    args = [nc.dram_tensor(k, v.shape, F32, kind="ExternalInput").ap() for k, v in arrays.items()]
    mixed = nc.dram_tensor("mixed", [KT, P, T], F32, kind="Internal").ap()
    out = nc.dram_tensor("out", [T, D], F32, kind="ExternalOutput").ap()
    build(nc, *args, mixed, out)
    r = run_bass_kernel_spmd(nc, [arrays], core_ids=[0])
    y = r.results[0]["out"]
    return y[S_SAMPLE:][None], y[:S_SAMPLE][None]
```
